# Optimizing a Trainium2 kernel written in Bass

```python
import jax, jax.numpy as jnp
from jax import lax
import numpy as np

D_MODEL = 2048
BATCH = 1
SEQ = 1024
DEPTH = 1

GRID_W = 64
NA_HEADS = 8
NA_HEAD_DIM = 128
NA_WIDTH = NA_HEADS * NA_HEAD_DIM
NA_KR_MAX = 8
NA_KC = 16
ML_HEADS = 4
ML_QK_DIM = 128
ML_V_DIM = 256
ML_QK_WIDTH = ML_HEADS * ML_QK_DIM
ML_V_WIDTH = ML_HEADS * ML_V_DIM
ML_CHUNK = 64
CONV_W = 5
N_GATES = 4 * ML_HEADS
D_MIX = NA_WIDTH + ML_V_WIDTH
N_IN = 3 * NA_WIDTH + 2 * ML_QK_WIDTH + 2 * ML_V_WIDTH + N_GATES
IN_SPLITS = (NA_WIDTH, 2 * NA_WIDTH, 3 * NA_WIDTH,
             3 * NA_WIDTH + ML_QK_WIDTH,
             3 * NA_WIDTH + 2 * ML_QK_WIDTH,
             3 * NA_WIDTH + 2 * ML_QK_WIDTH + ML_V_WIDTH,
             3 * NA_WIDTH + 2 * ML_QK_WIDTH + 2 * ML_V_WIDTH)
N_EXPERTS = 16
CAPACITY_FACTOR = 2
D_EXPERT = 1024
EPS = 1e-6

kernel_name = 'hybrid_na_mlstm_ec_encoder'

def rmsnorm(x, g):
    xf = x.astype(jnp.float32)
    y = xf * lax.rsqrt(jnp.mean(xf * xf, axis=-1, keepdims=True) + EPS)
    return (y * g.astype(jnp.float32)).astype(x.dtype)

def neighbourhood_attention(q, k, v, rpb):
    B, S, _ = q.shape
    H, d = NA_HEADS, NA_HEAD_DIM
    rows = S // GRID_W
    kr = min(NA_KR_MAX, rows)
    r = np.arange(rows)
    row_start = np.clip(r - kr // 2, 0, rows - kr)
    key_rows = row_start[:, None] + np.arange(kr)[None, :]
    c = np.arange(GRID_W)
    col_start = np.clip(c - NA_KC // 2, 0, GRID_W - NA_KC)
    col_in = (c[None, :] >= col_start[:, None]) & (c[None, :] < col_start[:, None] + NA_KC)
    dr = key_rows - r[:, None] + (NA_KR_MAX - 1)
    dc = np.clip(c[None, :] - c[:, None] + (NA_KC - 1), 0, 2 * NA_KC - 2)

    qg = q.reshape(B, rows, GRID_W, H, d)
    kg = k.reshape(B, rows, GRID_W, H, d)[:, key_rows]
    vg = v.reshape(B, rows, GRID_W, H, d)[:, key_rows]
    s = jnp.einsum('brqhd,brakhd->bhrqak', qg, kg,
                   preferred_element_type=jnp.float32) * (d ** -0.5)
    bias = rpb[:, dr[:, None, :, None], dc[None, :, None, :]]
    s = s + bias[None].astype(jnp.float32)
    s = jnp.where(col_in[None, None, None, :, None, :], s, -jnp.inf)
    p = jax.nn.softmax(s.reshape(B, H, rows, GRID_W, kr * GRID_W), axis=-1).reshape(s.shape)
    o = jnp.einsum('bhrqak,brakhd->brqhd', p.astype(v.dtype), vg)
    return o.reshape(B, S, H * d)

def mlstm_chunkwise(q, k, v, i_pre, f_pre):
    B, H, S, dk = q.shape
    dv = v.shape[-1]
    L = ML_CHUNK
    nc = S // L
    q = q * (dk ** -0.5)
    log_f = jax.nn.log_sigmoid(f_pre)

    def to_chunks(a):
        return jnp.moveaxis(a.reshape((B, H, nc, L) + a.shape[3:]), 2, 0)

    xs = (to_chunks(q), to_chunks(k), to_chunks(v), to_chunks(i_pre), to_chunks(log_f))
    lower = jnp.tril(jnp.ones((L, L), dtype=bool))

    def step(carry, inp):
        C, n, m = carry
        qb, kb, vb, ib, fb = inp
        b = jnp.cumsum(fb, axis=-1)
        dmat = b[..., :, None] - b[..., None, :] + ib[..., None, :]
        dmat = jnp.where(lower, dmat, -jnp.inf)
        m_inter = b + m[..., None]
        m_j = jnp.maximum(m_inter, jnp.max(dmat, axis=-1))
        w = jnp.exp(dmat - m_j[..., None])
        inter = jnp.exp(m_inter - m_j)
        qk = jnp.einsum('bhjd,bhsd->bhjs', qb, kb) * w
        num = inter[..., None] * jnp.einsum('bhjd,bhde->bhje', qb, C) + jnp.einsum('bhjs,bhse->bhje', qk, vb)
        den = inter * jnp.einsum('bhjd,bhd->bhj', qb, n) + jnp.sum(qk, axis=-1)
        h = num / jnp.maximum(jnp.abs(den), jnp.exp(-m_j))[..., None]
        b_last = b[..., -1]
        g = b_last[..., None] - b + ib
        m_new = jnp.maximum(b_last + m, jnp.max(g, axis=-1))
        decay = jnp.exp(b_last + m - m_new)
        wk = jnp.exp(g - m_new[..., None])
        C_new = decay[..., None, None] * C + jnp.einsum('bhs,bhsd,bhse->bhde', wk, kb, vb)
        n_new = decay[..., None] * n + jnp.einsum('bhs,bhsd->bhd', wk, kb)
        return (C_new, n_new, m_new), h

    init = (jnp.zeros((B, H, dk, dv), jnp.float32),
            jnp.zeros((B, H, dk), jnp.float32),
            jnp.zeros((B, H), jnp.float32))
    _, hs = lax.scan(step, init, xs)
    return jnp.moveaxis(hs, 0, 2).reshape(B, H, S, dv)

def mlstm_mixer(ml_q, ml_k, ml_v, ml_o, gates, b_gates, conv_w, conv_b, norm_g):
    B, S, _ = ml_q.shape
    H = ML_HEADS
    qk = jnp.concatenate([ml_q, ml_k], axis=-1)
    qk = lax.conv_general_dilated(qk, conv_w[:, None, :], (1,), [(CONV_W // 2, CONV_W // 2)],
                                  dimension_numbers=('NWC', 'WIO', 'NWC'),
                                  feature_group_count=2 * ML_QK_WIDTH) + conv_b
    qk = jax.nn.silu(qk)
    q, k = jnp.split(qk, 2, axis=-1)

    def heads(a, dh):
        return jnp.transpose(a.reshape(B, S, H, dh), (0, 2, 1, 3)).astype(jnp.float32)

    q, k, v = heads(q, ML_QK_DIM), heads(k, ML_QK_DIM), heads(ml_v, ML_V_DIM)
    g = gates.astype(jnp.float32) + b_gates.astype(jnp.float32)
    g = jnp.transpose(g.reshape(B, S, 4, H), (2, 0, 3, 1))
    h_fwd = mlstm_chunkwise(q, k, v, g[0], g[1])
    flip = lambda a: jnp.flip(a, axis=2)
    h_bwd = flip(mlstm_chunkwise(flip(q), flip(k), flip(v), flip(g[2]), flip(g[3])))
    h = h_fwd + h_bwd
    h = h * lax.rsqrt(jnp.mean(h * h, axis=-1, keepdims=True) + EPS)
    h = jnp.transpose(h, (0, 2, 1, 3)).reshape(B, S, ML_V_WIDTH) * norm_g.astype(jnp.float32)
    return (h * jax.nn.sigmoid(ml_o.astype(jnp.float32))).astype(ml_v.dtype)

def expert_choice_ffn(h, w_router, w_gate, w_up, w_down):
    B, S, _ = h.shape
    cap = CAPACITY_FACTOR * S // N_EXPERTS
    logits = jnp.einsum('bsd,de->bse', h, w_router, preferred_element_type=jnp.float32)
    aff = jax.nn.softmax(logits, axis=-1)
    gate, tok = lax.top_k(jnp.swapaxes(aff, 1, 2), cap)
    bidx = jnp.arange(B)[:, None, None]
    xin = h[bidx, tok]
    a = jnp.einsum('becd,edf->becf', xin, w_gate)
    u = jnp.einsum('becd,edf->becf', xin, w_up)
    y = jnp.einsum('becf,efd->becd', jax.nn.silu(a) * u, w_down)
    y = y * gate[..., None].astype(y.dtype)
    return jnp.zeros_like(h).at[bidx, tok].add(y)

def setup_inputs(seed: int = 0) -> dict:
    key = jax.random.key(seed)
    ks = jax.random.split(key, 16)
    f32 = jnp.float32

    def nrm(k, shape, scale):
        return jax.random.normal(k, shape, f32) * scale

    fb = jnp.linspace(3.0, 6.0, ML_HEADS, dtype=f32)
    zb = jnp.zeros((ML_HEADS,), f32)
    gate_base = jnp.concatenate([zb, fb, zb, fb])
    return {
        'x': nrm(ks[0], (BATCH, SEQ, D_MODEL), 1.0),
        'norm_mix_g': 1.0 + nrm(ks[1], (DEPTH, D_MODEL), 0.02),
        'w_in': nrm(ks[2], (DEPTH, D_MODEL, N_IN), D_MODEL ** -0.5),
        'b_gates': gate_base[None, :] + nrm(ks[3], (DEPTH, N_GATES), 0.1),
        'conv_w': nrm(ks[4], (DEPTH, CONV_W, 2 * ML_QK_WIDTH), CONV_W ** -0.5),
        'conv_b': nrm(ks[5], (DEPTH, 2 * ML_QK_WIDTH), 0.02),
        'na_rpb': nrm(ks[6], (DEPTH, NA_HEADS, 2 * NA_KR_MAX - 1, 2 * NA_KC - 1), 0.1),
        'na_norm_g': 1.0 + nrm(ks[7], (DEPTH, NA_WIDTH), 0.02),
        'ml_norm_g': 1.0 + nrm(ks[8], (DEPTH, ML_V_WIDTH), 0.02),
        'w_out': nrm(ks[9], (DEPTH, D_MIX, D_MODEL), D_MIX ** -0.5),
        'norm_ffn_g': 1.0 + nrm(ks[10], (DEPTH, D_MODEL), 0.02),
        'w_router': nrm(ks[11], (DEPTH, D_MODEL, N_EXPERTS), D_MODEL ** -0.5),
        'w_gate': nrm(ks[12], (DEPTH, N_EXPERTS, D_MODEL, D_EXPERT), D_MODEL ** -0.5),
        'w_up': nrm(ks[13], (DEPTH, N_EXPERTS, D_MODEL, D_EXPERT), D_MODEL ** -0.5),
        'w_down': nrm(ks[14], (DEPTH, N_EXPERTS, D_EXPERT, D_MODEL), D_EXPERT ** -0.5),
        'final_norm_g': 1.0 + nrm(ks[15], (D_MODEL,), 0.02),
    }

def reference(x, norm_mix_g, w_in, b_gates, conv_w, conv_b, na_rpb, na_norm_g, ml_norm_g,
              w_out, norm_ffn_g, w_router, w_gate, w_up, w_down, final_norm_g):
    for l in range(DEPTH):
        h = rmsnorm(x, norm_mix_g[l])
        proj = jnp.einsum('bsd,dn->bsn', h, w_in[l])
        na_q, na_k, na_v, ml_q, ml_k, ml_v, ml_o, gates = jnp.split(proj, IN_SPLITS, axis=-1)
        na_out = rmsnorm(neighbourhood_attention(na_q, na_k, na_v, na_rpb[l]), na_norm_g[l])
        ml_out = mlstm_mixer(ml_q, ml_k, ml_v, ml_o, gates, b_gates[l], conv_w[l], conv_b[l], ml_norm_g[l])
        mix = jnp.concatenate([na_out, ml_out], axis=-1)
        x = x + jnp.einsum('bsm,md->bsd', mix, w_out[l])
        h = rmsnorm(x, norm_ffn_g[l])
        x = x + expert_choice_ffn(h, w_router[l], w_gate[l], w_up[l], w_down[l])
    return rmsnorm(x, final_norm_g)


_drawn_inputs = setup_inputs


def setup_inputs(seed=0):
    import zlib

    import numpy as np

    out = dict(_drawn_inputs(seed))
    spreads = {}
    factors = {'conv_b': 6.63,
     'na_norm_g': 3.956,
     'ml_norm_g': 7.227,
     'norm_ffn_g': 4.26,
     'final_norm_g': 2.749}
    for name, (base, spread) in spreads.items():
        noise = np.random.default_rng([zlib.crc32(name.encode()), seed]).standard_normal(out[name].shape)
        drawn = base * np.exp(spread * noise) if base else spread * noise
        out[name] = __import__('jax').numpy.asarray(drawn.astype(out[name].dtype))
    for name, factor in factors.items():
        out[name] = (out[name] * factor).astype(out[name].dtype)
    return out
```

```python
import math
from contextlib import ExitStack

import numpy as np

import concourse.bass as bass
from concourse import mybir
from concourse.alu_op_type import AluOpType as ALU

F32 = mybir.dt.float32
F32R = mybir.dt.float32r
U32 = mybir.dt.uint32
ACT = mybir.ActivationFunctionType
AX = mybir.AxisListType

P = 128
SEQ, D = 1024, 2048
TT = SEQ // P
KD = D // P
NAH, HD = 8, 128
GW = 64
ROWS = SEQ // GW
KR, KC = 8, 16
MLH, DK, DV = 4, 128, 256
CONVW = 5
NE, CAP, DE = 16, 128, 1024
KE = DE // P
EPS = 1e-6
NEG = -1e30
BW = 512
BLK = 12
ROWBLK = 6
OBLK = 4
CPB = KD // 2
RING = 4
LNS = -0.5 * math.log(DK)
TOPR = CAP // 8
ERAW, ESPL = 8, 8
EPC = 2 * KD + 2 * KE


class Steps:

    def __init__(self, eng, sem, past=None):
        self.eng, self.sem, self.done, self.inside, self.turn, self.per = eng, sem, 0, 0, None, 0
        self.past = past or eng.wait_ge

    def enter(self, turn, per):
        self.turn, self.per, self.inside = turn, per, 0

    def leave(self, turns):
        assert self.inside == self.per, (self.inside, self.per)
        self.done, self.turn, self.inside = self.done + turns * self.per, None, 0

    def settle(self):
        if self.turn is None:
            self.done += 1
            self.eng.wait_ge(self.sem, self.done)
        else:
            self.inside += 1
            self.past(self.sem, self.turn * self.per + (self.done + self.inside))


def trunk(nc, t):
    ctx = ExitStack()
    with ctx:
        def sb(name, shape, dt=F32, stack=None):
            return (stack or ctx).enter_context(nc.sbuf_tensor(name, shape, dt))

        def sem(name):
            return ctx.enter_context(nc.semaphore(name))

        ident = sb("ident", [P, P])
        nag = sb("nag", [P, NAH])
        mlg = sb("mlg", [P, NAH])
        pad = sb("pad", [NAH * 15, 2 * GW - 1])
        half = sb("half", [P, 8])
        meansq = sb("meansq", [P, 8])
        rstd = sb("rstd", [P, 8])
        msq = sb("msq", [P, 2, 5])
        rs = sb("rs", [P, 2, 5])
        cols = sb("cols", [P, TT, 4, 2, MLH])
        decbc = sb("decbc", [P, 2, MLH, TT])

        proj = ExitStack()
        raw = sb("raw", [P, RING, 1024], F32, proj)
        whi = sb("whi", [P, RING, 1024], F32R, proj)
        wlo = sb("wlo", [P, RING, 1024], F32R, proj)
        stage = sb("stage", [P, 4, BW], F32, proj)
        t0 = sb("t0", [P, 1024], F32, proj)
        t1 = sb("t1", [P, 1024], F32, proj)
        t2 = sb("t2", [P, 1028], F32, proj)
        rstd_bc = sb("rstd_bc", [P, 1024], F32, proj)
        t3 = stage[:, 0:2, :].rearrange("p a b -> p (a b)")
        wide = ExitStack()
        a_hi = sb("a_hi", [P, KD, SEQ], F32R, wide)
        a_lo = sb("a_lo", [P, KD, SEQ], F32R, wide)
        gmix = sb("gmix", [P, KD], F32, wide)
        ssum = sb("ssum", [P, KD], F32, wide)
        wg_raw = sb("wg_raw", [P, KD, 16], F32, wide)
        wg = sb("wg", [P, KD, 32], F32R, wide)
        wide.close()
        gate = ExitStack()
        _skip = gate.enter_context(nc.sbuf_tensor("skip_a", [P, 2 * KD * SEQ], F32))
        _skip2 = gate.enter_context(nc.sbuf_tensor("skip_b", [P, 2 * KD + KD * 16 + KD * 32], F32))
        g_two = sb("g_two", [P, TT, 32], F32, gate)
        g_nat = sb("g_nat", [P, TT, 16], F32, gate)
        g_bias = sb("g_bias", [P, 16], F32, gate)
        b_last = sb("b_last", [64, TT], F32, gate)
        c_last = sb("c_last", [64, TT], F32, gate)
        m_next = sb("m_next", [64, TT + 2], F32, gate)
        m_prev = sb("m_prev", [64, TT], F32, gate)
        m_end = sb("m_end", [64, TT], F32, gate)
        decay = sb("decay", [64, TT], F32, gate)
        cw = sb("cw", [P, 2, CONVW + 1], F32, gate)
        gate.close()

        nbh = ExitStack()
        na_out = sb("na_out", [P, TT, NAH * HD], F32, nbh)
        naq = sb("naq", [P, 2, SEQ], F32, nbh)
        nak = sb("nak", [P, 2, SEQ], F32, nbh)
        nav = sb("nav", [P, 2, TT, HD], F32, nbh)
        bias = sb("bias", [P, 2, 14, GW], F32, nbh)
        bias9 = sb("bias9", [P, 2, 9, GW], F32, nbh)
        prob = sb("prob", [P, 2, 9 * GW], F32, nbh)
        probT = sb("probT", [P, 2, 5, P], F32, nbh)
        top = sb("top", [P, 2], F32, nbh)
        ntop = sb("ntop", [P, 2], F32, nbh)
        psumr = sb("psumr", [P, 2], F32, nbh)
        pinv = sb("pinv", [P, 2], F32, nbh)
        qrows = sb("qrows", [P, 2, SEQ], F32, nbh)
        nbh.close()
        mls = ExitStack()
        _skip3 = mls.enter_context(nc.sbuf_tensor("skip_c", [P, TT * NAH * HD], F32))
        mq = sb("mq", [P, 2, SEQ], F32, mls)
        mk = sb("mk", [P, 2, SEQ], F32, mls)
        mv = sb("mv", [P, 2, TT, DV + 1], F32, mls)
        mbc = sb("mbc", [P, 2, 2, SEQ], F32, mls)
        kn = sb("kn", [P, TT, DK], F32, mls)
        st = sb("st", [P, SEQ], F32, mls)
        wexp = sb("wexp", [P, 2, P], F32, mls)
        kw = sb("kw", [P, 2, DK], F32, mls)
        qkw = sb("qkw", [P, 2, P], F32, mls)
        inter = sb("inter", [P, 2, DV + 1], F32, mls)
        hsum = sb("hsum", [P, 2, DV + 1], F32, mls)
        cst = sb("cst", [P, 2, DV + 1], F32, mls)
        den = sb("den", [P, 2], F32, mls)
        hcols = sb("hcols", [P, 2, TT, 4, 2], F32, mls)
        hdec = sb("hdec", [P, 2, 2, TT], F32, mls)
        mh = sb("mh", [P, 2, TT, DV], F32, mls)
        mls.close()
        proj.close()

        exps = ExitStack()
        rx = sb("rx", [P, 2, D], F32, exps)
        rh = sb("rh", [P, 2, D], F32, exps)
        gbc = sb("gbc", [P, D], F32, exps)
        rT = sb("rT", [P, KD, P], F32, exps)
        wr = sb("wr", [P, KD, NE], F32, exps)
        rsmall = sb("rsmall", [P, 4], F32, exps)
        affT = sb("affT", [NE, SEQ], F32, exps)
        best = sb("best", [NE, CAP], F32, exps)
        besti = sb("besti", [NE, CAP], U32, exps)
        bestf = sb("bestf", [NE, CAP], F32, exps)
        gateT = sb("gateT", [P, NE], F32, exps)
        tokT = sb("tokT", [P, NE], U32, exps)
        tokg = sb("tokg", [P, 1], U32, exps)
        toks = sb("toks", [P, 1], U32, exps)
        gcol = sb("gcol", [P, 1], F32, exps)
        smx = sb("smx", [P, TT], F32, exps)
        affs = sb("affs", [P, TT, NE], F32, exps)
        eraw = sb("eraw", [P, ERAW, 1024], F32, exps)
        ehi = sb("ehi", [P, ESPL, 1024], F32R, exps)
        elo = sb("elo", [P, ESPL, 1024], F32R, exps)
        exps.close()
        exp2 = ExitStack()
        xg = sb("xg", [P, D], F32, exp2)
        xh = sb("xh", [P, KD, P], F32R, exp2)
        xl = sb("xl", [P, KD, P], F32R, exp2)
        hact = sb("hact", [P, DE], F32, exp2)
        hh = sb("hh", [P, KE, P], F32R, exp2)
        hl = sb("hl", [P, KE, P], F32R, exp2)
        ey = sb("ey", [P, D], F32, exp2)
        exp2.close()

        ps = ctx.enter_context(nc.psum_tensor("ps", [P, 8, BW], F32))

        S = {}
        for n in ("const_in ident_done raw0 raw1 raw2 raw3 xt0 xt1 xnat xn_sq hT_hi hT_lo w_hi w_lo w_used "
                  "bank_ready bank_staged st0 st1 st2 st3 stage_free meansq_done rstd_done rstd_out rstd_bc_in "
                  "wg_hi wg_done gates_ready gates_copied gpad_zero gpad_done grows_ready grows_out dve_step "
                  "act_step pool_step mask_done acc_free conv_in conv_free silu_done conv_out feats_out x1_init "
                  "pool_past dve_past pad_in rep_out cols_ready cols_out nq0 nq1 nkv0 nkv1 nb0 nb1 q_scaled "
                  "bias_ready qk_done scored na_max exp_done transposed pt_evicted pv_done na_step na_out_done "
                  "na_saved ml0 ml1 hcols_ready kn_ready kn_out st_ready st_out wexp_done masked kw_done qkw_done "
                  "kv_done num_done xa0 xa1 rs_done asm_stats asm_mean asm_scaled asm_tr mixT_hi mixT_lo x1_done "
                  "rc_in rx0 rx1 r_sq r_mean r_rstd r_norm rh_free r_tr r_tA r_tD r_logit smax r_exp affn aff_tr "
                  "aff_out best_out er4 er5 er6 er7 e_hi e_lo e_used gu_ready silu2 hmul xtr x_hi x_lo htr h_hi "
                  "h_lo y_ready y_out tokg_done toks_done gcol_done gathered scattered ey_free intr_done t_done "
                  "c_zeroed c_updated hs_done ml_head_done ml_saved mh_free ones_done gate_act gate_arg gate_out "
                  "gates_in h_out").split():
            S[n] = sem(n)
        rawsem = [S[f"raw{i}"] for i in range(4)]
        stsem = [S[f"st{i}"] for i in range(4)]
        xtsem = [S["xt0"], S["xt1"]]
        xasem, rxsem = ([S[n + "0"], S[n + "1"]] for n in ("xa", "rx"))
        ersem = rawsem + [S[f"er{i}"] for i in range(RING, ERAW)]
        ER0 = [32 * (BLK + OBLK)] * RING + [0] * (ERAW - RING)
        nqsem, nkvsem, nbsem, mlsem = ([S[n + "0"], S[n + "1"]] for n in ("nq", "nkv", "nb", "ml"))
        KEY0 = [0, 0, 0, 1, 2, 3, 4, 4]
        BROW = [7, 5, 3, 3, 3, 3, 3, 1]
        WIDE = [8 * GW, 8 * GW] + [9 * GW] * 4 + [8 * GW, 8 * GW]

        def flat2(a):
            return a.rearrange("p a b -> p (a b)")

        SC = [flat2(ps[:, 0:2, :]), flat2(ps[:, 2:4, :])]
        PTP = flat2(ps[:, 4:6, :])

        mixA = [t0[:, :], flat2(stage[:, 0:2, :])]
        mixB = [t1[:, :], flat2(stage[:, 2:4, :])]
        mixO = [t2[:, 0:1024], rstd_bc[:, :]]

        def used(e, j):
            if j in (30, 31):
                return S["gu_ready"], e + 1
            if j in (46, 47):
                return S["y_ready"], 4 * e + 4
            return S["e_used"], 44 * e + (j + 1 if j < 30 else j - 1)

        def ml_unit(u):
            return (u // 2, 0) if u % 2 == 0 else (TT - 1 - u // 2, 1)

        def chunk_free(eng, b, m):
            if m >= 4:
                eng.wait_ge(S["w_used"], 7 * b + (m - 3))
            elif m < 3:
                eng.wait_ge(S["w_used"], 7 * b + (m - 2))
            else:
                eng.wait_ge(S["bank_ready"], 8 * b)

        block = ctx.enter_context(nc.Block())

        @block.sync
        def _(sp):
            def fetch(b, m):
                if not (isinstance(b, int) and b == 0 and m < 4):
                    sp.wait_ge(S["w_lo"], CPB * b + (m - 3))
                src = t["w_stream"][bass.ds(CPB * b + m, 1), :, :].rearrange("a p c -> (a p) c")
                sp.dma_start(raw[:, m % RING, :], src).then_inc(rawsem[m % RING], 16)

            for m in range(CPB):
                fetch(0, m)
                for k in (2 * m, 2 * m + 1):
                    if k >= 2:
                        sp.wait_ge(S["hT_lo"], k - 1)
                    sp.dma_start((t0, t1)[k % 2][:, :], t["xT"][k * P:(k + 1) * P, :]).then_inc(xtsem[k % 2], 16)
            with sp.Fori(1, BLK) as b:
                for m in range(CPB):
                    fetch(b, m)
            for m in range(RING):
                fetch(BLK, m)

            sp.wait_ge(S["bank_ready"], 8 * BLK)
            sp.wait_ge(S["feats_out"], 1)
            sp.dma_start(qrows[:, :, :], t["q_rows"].rearrange("a p c -> p a c")).then_inc(S["gates_in"], 16)
            sp.dma_start(decbc[:, :, :, :].rearrange("p d h n -> p (d h n)"),
                         t["decays"].rearrange("a n -> (a n)").partition_broadcast(P)).then_inc(S["gates_in"], 16)

            def fetch_head(i, hb):
                feats = t["feats"]
                q = feats[bass.ds(2 * i + (hb + 8), 1), :, :].rearrange("a p c -> (a p) c")
                k = feats[bass.ds(2 * i + (hb + 16), 1), :, :].rearrange("a p c -> (a p) c")
                v = t["rows"].rearrange("(n p) c -> p n c", p=P)[:, :, bass.ds((2 * i + hb) * HD, HD)]
                sp.dma_start(naq[:, hb, :], q).then_inc(nqsem[hb], 16)
                sp.dma_start(nak[:, hb, :], k).then_inc(nkvsem[hb], 16)
                sp.dma_start(nav[:, hb, :, :], v).then_inc(nkvsem[hb], 16)

            fetch_head(0, 0)
            fetch_head(0, 1)
            with sp.Fori(1, NAH // 2) as i:
                for hb in range(2):
                    sp.wait_ge(S["pv_done"], 16 * i + (8 * hb - 8 + 2))
                    fetch_head(i, hb)
            sp.wait_ge(S["na_out_done"], 64 + 2)
            sp.dma_start(t["na"].rearrange("(n p) c -> p n c", p=P), na_out[:, :, :]).then_inc(S["na_saved"], 16)

            def fetch_ml(h):
                hb = h % 2
                sp.dma_start(mq[:, hb, :], t["conv"][h, :, :]).then_inc(mlsem[hb], 16)
                sp.dma_start(mk[:, hb, :], t["conv"][MLH + h, :, :]).then_inc(mlsem[hb], 16)
                sp.dma_start(mv[:, hb, :, 0:DV], t["rows"].rearrange("(n p) c -> p n c", p=P)
                             [:, :, 1024 + h * DV:1024 + (h + 1) * DV]).then_inc(mlsem[hb], 16)
                for d in range(2):
                    sp.dma_start(mbc[:, hb, d, :], t["m_rows"][d * MLH + h, :].partition_broadcast(P)).then_inc(mlsem[hb], 16)

            sp.sem_inc(S["mh_free"], 2)
            fetch_ml(0)
            fetch_ml(1)
            for h in range(MLH):
                sp.wait_ge(S["ml_head_done"], h + 1)
                sp.dma_start(t["ml"].rearrange("(n p) c -> p n c", p=P)[:, :, h * DV:(h + 1) * DV], mh[:, h % 2, :, :])\
                    .then_inc(S["ml_saved"], 16)
                sp.wait_ge(S["ml_saved"], 16 * (h + 1))
                sp.sem_inc(S["mh_free"], 1)
                if h + 2 < MLH:
                    fetch_ml(h + 2)

            sp.wait_ge(S["na_saved"], 16)

            def fetch_mix(i, p):
                rows = bass.ds((2 * i + p) * P, P)
                sp.dma_start(mixA[p], t["na"][rows, :]).then_inc(xasem[p], 16)
                sp.dma_start(mixB[p], t["ml"][rows, :]).then_inc(xasem[p], 16)
                sp.dma_start(mixO[p], t["rows"][rows, 2048:3072]).then_inc(xasem[p], 16)

            fetch_mix(0, 0)
            fetch_mix(0, 1)
            with sp.Fori(1, TT // 2) as i:
                for p in range(2):
                    sp.wait_ge(S["asm_tr"], 8 * i + (4 * p - 4))
                    fetch_mix(i, p)
            for m in range(RING, CPB):
                fetch(BLK, m)
            with sp.Fori(BLK + 1, BLK + OBLK) as b:
                for m in range(CPB):
                    fetch(b, m)

            sp.wait_ge(S["bank_ready"], 8 * (BLK + OBLK))
            sp.wait_ge(S["x1_done"], 1)
            sp.dma_start(gbc[:, :], t["g_ffn"].partition_broadcast(P)).then_inc(S["rc_in"], 16)
            sp.dma_start(wr[:, :, :], t["w_router"]).then_inc(S["rc_in"], 16)

            def fetch_x1(i, p, base):
                sp.dma_start(rx[:, p, :], t["x1"][bass.ds((2 * i + (p - base)) * P, P), :]).then_inc(rxsem[p], 16)

            def fetch_piece(e, j):
                if not (isinstance(e, int) and j < ERAW):
                    sp.wait_ge(S["e_lo"], EPC * e + (j - ERAW + 1))
                k = j // 2 if j < 2 * KD else (j - 2 * KD) // 2
                if j < 2 * KD:
                    src = t[("w_gate", "w_up")[j % 2]][bass.ds(e, 1), k * P:(k + 1) * P, :]
                else:
                    src = t["w_down"][bass.ds(e, 1), k * P:(k + 1) * P, (j % 2) * 1024:(j % 2 + 1) * 1024]
                sp.dma_start(eraw[:, j % ERAW, :], src.rearrange("a p c -> (a p) c")).then_inc(ersem[j % ERAW], 16)

            sp.sem_inc(S["rh_free"], 2)
            fetch_x1(0, 0, 0)
            fetch_x1(0, 1, 0)
            for j in range(ERAW):
                fetch_piece(0, j)

            def norm_io(i, dst, last, base):
                for p in range(2):
                    sp.wait_ge(S["r_norm"], 2 * i + (p + 1))
                    sp.dma_start(t[dst][bass.ds((2 * i + (p - base)) * P, P), :], rh[:, p, :]).then_inc(S["h_out"], 16)
                    if not last:
                        fetch_x1(i + 1, p, base)
                    sp.wait_ge(S["h_out"], 32 * i + (16 * p + 16))
                    sp.sem_inc(S["rh_free"], 1)

            with sp.Fori(0, TT // 2 - 1) as i:
                norm_io(i, "h2", False, 0)
            norm_io(TT // 2 - 1, "h2", True, 0)

            for j in range(ERAW, EPC):
                fetch_piece(0, j)
            with sp.Fori(1, NE) as e:
                for j in range(EPC):
                    fetch_piece(e, j)

            sp.wait_ge(S["ey_free"], NE + 1)
            sp.dma_start(gbc[:, :], t["g_final"].partition_broadcast(P)).then_inc(S["rc_in"], 16)
            fetch_x1(TT // 2, 0, TT)
            fetch_x1(TT // 2, 1, TT)
            with sp.Fori(TT // 2, TT - 1) as i:
                norm_io(i, "out", False, TT)
            norm_io(TT - 1, "out", True, TT)
            sp.wait_ge(S["h_out"], 16 * 2 * TT)

        @block.gpsimd
        def _(pool):
            def past(s, v):
                pool.wait_ge(s, v)
                pool.sem_inc(S["pool_past"], 1)

            step = Steps(pool, S["pool_step"], past)

            pool.memset(ident[:, :], 0.0).then_inc(S["pool_step"], 1)
            step.settle()
            pool.affine_select(out=ident[:, :], in_=ident[:, :], compare_op=ALU.not_equal, fill=1.0, base=0,
                               pattern=[[-1, P]], channel_multiplier=1).then_inc(S["ident_done"], 1)
            pool.memset(half[:, :], -0.5).then_inc(S["pool_step"], 1)
            step.settle()
            pool.memset(pad[:, :], NEG).then_inc(S["pool_step"], 1)
            step.settle()
            pool.dma_start(pad[:, GW - KC:GW + KC - 1], t["rpb"].rearrange("h r c -> (h r) c")).then_inc(S["pad_in"], 16)
            for dst, src in ((gmix[:, :], t["g_mix"]), (wg_raw[:, :, :], t["w_gates"]),
                             (g_bias[:, :], t["b_gates"].partition_broadcast(P)),
                             (nag[:, :], t["na_g"]), (mlg[:, :], t["ml_g"])):
                pool.dma_start(dst, src).then_inc(S["const_in"], 16)
            pool.wait_ge(S["pad_in"], 16)
            pool.dma_start(t["rpb_rep"].rearrange("h r c j -> (h r) c j"),
                           pad[:, :].unsqueeze(1).broadcast_to([NAH * 15, GW, 2 * GW - 1])).then_inc(S["rep_out"], 16)
            for k in range(KD):
                if k:
                    pool.wait_ge(S["xn_sq"], k)
                pool.dma_start(t2[:, 0:1024], t["x"][(k // 2) * P:(k // 2 + 1) * P,
                                                     (k % 2) * 1024:(k % 2 + 1) * 1024]).then_inc(S["xnat"], 16)
            pool.wait_ge(S["meansq_done"], 1)
            pool.tensor_tensor(rstd[:, :], meansq[:, :], half[:, :], ALU.pow).then_inc(S["rstd_done"], 1)
            pool.wait_ge(S["rstd_done"], 1)
            pool.dma_start(t["rstd_d"].rearrange("(t p) -> p t", p=P), rstd[:, :],
                           allow_slow_non_contiguous=True).then_inc(S["rstd_out"], 16)
            pool.wait_ge(S["rstd_out"], 16)
            pool.dma_start(rstd_bc[:, :], t["rstd_d"].partition_broadcast(P)).then_inc(S["rstd_bc_in"], 16)
            pool.wait_ge(S["xn_sq"], KD)
            pool.memset(t2[:, 0:1024], 0.0).then_inc(S["gpad_zero"], 1)
            for s in (b_last, c_last, m_prev):
                pool.memset(s[:, :], 0.0).then_inc(S["gpad_zero"], 1)
            pool.memset(m_next[:, :], 0.0).then_inc(S["gpad_zero"], 1)

            def store(b, dst, accum=False):
                for n in range(8):
                    past(S["bank_staged"], 8 * b + (n + 1))
                    if accum:
                        pool.dma_start(dst(b, n), stage[:, n % 4, :], accum_op=ALU.add).then_inc(stsem[n % 4], 16)
                    else:
                        pool.dma_start(dst(b, n), stage[:, n % 4, :]).then_inc(stsem[n % 4], 16)
                    for o in (n - 2,) if n < 7 else (5, 6, 7):
                        if o >= 0:
                            past(stsem[o % 4], 32 * b + 16 * (o // 4 + 1))
                            pool.sem_inc(S["stage_free"], 1)

            def to_rows(b, n):
                return t["rows"][n * P:(n + 1) * P, bass.ds(b * BW, BW)]

            def to_feats(b, n):
                g, hh_ = n // 2, n % 2
                return t["feats"][bass.ds(4 * b + (g - 4 * ROWBLK), 1), :, hh_ * BW:(hh_ + 1) * BW]\
                    .rearrange("a p c -> (a p) c")

            with pool.Fori(0, ROWBLK) as b:
                store(b, to_rows)

            pool.memset(t3, 1.0).then_inc(S["pool_step"], 1)
            step.settle()
            pool.memset(t3.rearrange("p (n j) -> p n j", j=P)[:, :, 0:1], 0.0).then_inc(S["mask_done"], 1)
            pool.wait_ge(S["gate_act"], 5)
            for d in range(2):
                pool.dma_start(t["m_rows"][d * MLH:(d + 1) * MLH, :], t2[32 * d:32 * d + MLH, 0:1024]).then_inc(S["gate_out"], 16)
                pool.dma_start(t["decays"][d * MLH:(d + 1) * MLH, :], decay[32 * d:32 * d + MLH, :]).then_inc(S["gate_out"], 16)
            pool.dma_start(t["q_rows"][0, :, :], t0[:, :]).then_inc(S["gate_out"], 16)
            pool.dma_start(t["q_rows"][1, :, :], t1[:, :]).then_inc(S["gate_out"], 16)
            pool.wait_ge(S["gate_out"], 96)
            pool.sem_inc(S["acc_free"], 1)
            for i in range(TT):
                pool.dma_start(t["x1"][i * P:(i + 1) * P, :], t["x"][i * P:(i + 1) * P, :]).then_inc(S["x1_init"], 16)

            with pool.Fori(ROWBLK, ROWBLK + 2) as b:
                store(b, to_feats)
            with pool.Fori(ROWBLK + 2, BLK) as b:
                for q in range(2):
                    c = 2 * b + (q - 2 * (ROWBLK + 2))
                    past(S["conv_free"], c + 1)
                    pool.dma_start(t2[:, 2:1026], t["feats"][bass.ds(c, 1), :, :].rearrange("a p c -> (a p) c"))\
                        .then_inc(S["conv_in"], 16)
                    pool.dma_start(cw[:, q, :], t["conv_wb"][bass.ds(c, 1), :, :].rearrange("a p c -> (a p) c"))\
                        .then_inc(S["conv_in"], 16)
                    past(S["silu_done"], c + 1)
                    pool.dma_start(t["conv"][bass.ds(c, 1), :, :].rearrange("a p c -> (a p) c"), t0[:, :])\
                        .then_inc(S["conv_out"], 16)
                    past(S["conv_out"], 16 * c + 16)
                    pool.sem_inc(S["acc_free"], 1)
                store(b, to_feats)
            pool.sem_inc(S["feats_out"], 1)

            pool.wait_ge(S["rep_out"], 16)

            def prepare(i, hb, first):
                h = 2 * i + hb
                if first:
                    pool.wait_ge(nqsem[hb], 16)
                else:
                    past(nqsem[hb], 16 * i + 16)
                pool.tensor_scalar(naq[:, hb, :], naq[:, hb, :], HD ** -0.5, 0.0, ALU.mult, ALU.add).then_inc(S["q_scaled"], 1)
                if not first:
                    past(S["scored"], 8 * h - 8 + 2)
                for r in range(2):
                    at = bass.AP(t["rpb_rep"].tensor, h * (15 * GW * 127) + ((1 - r) * GW * 127 + GW - 1),
                                 [[126, GW], [GW * 127, 14], [1, GW]])
                    pool.dma_start(bias[r * GW:(r + 1) * GW, hb, :, :], at).then_inc(nbsem[hb], 16)
                past(nbsem[hb], 32 * i + 32)
                for r in range(2):
                    rows = slice(r * GW, (r + 1) * GW)
                    a, b = bias[rows, hb, :, 0:GW - KC], bias[rows, hb, :, KC:GW]
                    pool.affine_select(out=a, in_=a, compare_op=ALU.is_ge, fill=NEG, base=KC // 2,
                                       pattern=[[0, 14], [1, GW - KC]], channel_multiplier=-1).then_inc(S["pool_step"], 1)
                    step.settle()
                    pool.affine_select(out=b, in_=b, compare_op=ALU.is_ge, fill=NEG, base=KC // 2 - 1 - KC,
                                       pattern=[[0, 14], [-1, GW - KC]], channel_multiplier=1).then_inc(S["pool_step"], 1)
                    step.settle()
                pool.tensor_copy(bias9[:, hb, :, :], bias[:, hb, 2:11, :]).then_inc(S["pool_step"], 1)
                step.settle()
                for r, a in enumerate((8, 0)):
                    pool.memset(bias9[r * GW:(r + 1) * GW, hb, a, :], NEG).then_inc(S["bias_ready"], 1)
                    if first:
                        pool.wait_ge(S["bias_ready"], 2 * hb + r + 1)
                    else:
                        past(S["bias_ready"], 4 * i + (2 * hb + r + 1))

            for hb in range(2):
                prepare(0, hb, True)
            with pool.Fori(1, NAH // 2) as i:
                step.enter(i - 1, 10)
                prepare(i, 0, False)
                prepare(i, 1, False)
                step.leave(NAH // 2 - 1)

            pool.wait_ge(S["na_out_done"], 64 + 2)
            for hb in range(2):
                pool.memset(mv[:, hb, :, DV:DV + 1], 1.0).then_inc(S["ones_done"], 1)
            pool.sem_inc(S["kw_done"], 1)
            with pool.Fori(0, MLH // 2) as i:
                for hb in range(2):
                    h = 2 * i + hb
                    past(S["kn_out"], 2 * h + 2)
                    past(S["hcols_ready"], 2 * h + 2)
                    for u in range(16):
                        n, d = ml_unit(u)
                        past(S["kv_done"], 16 * h + (u + 1))
                        pool.tensor_scalar(kw[:, u % 2, :], kn[:, n, :], hcols[:, hb, n, 1, d:d + 1], 0.0, ALU.mult, ALU.add)\
                            .then_inc(S["kw_done"], 1)
                        past(S["wexp_done"], 16 * h + (u + 1))
                        a = wexp[:, u % 2, :]
                        way = 1 if d == 0 else -1
                        pool.affine_select(out=a, in_=a, compare_op=ALU.is_ge, fill=0.0, base=0,
                                           pattern=[[way, P]], channel_multiplier=-way).then_inc(S["masked"], 1)

            with pool.Fori(0, TT // 2) as i:
                for p in range(2):
                    pool.wait_ge(S["asm_mean"], 2 * i + (p + 1))
                    pool.tensor_tensor(rs[:, p, :], msq[:, p, :], half[:, 0:5], ALU.pow).then_inc(S["rs_done"], 1)

            pool.wait_ge(S["x1_init"], 16 * TT)

            def to_x1(b, n):
                return t["x1"][n * P:(n + 1) * P, bass.ds((b - BLK) * BW, BW)]

            with pool.Fori(BLK, BLK + OBLK) as b:
                store(b, to_x1, accum=True)
            pool.sem_inc(S["x1_done"], 1)

            with pool.Fori(0, TT // 2) as i:
                for p in range(2):
                    pool.wait_ge(S["r_mean"], 2 * i + (p + 1))
                    pool.tensor_tensor(rstd[:, p:p + 1], rsmall[:, 2 + p:3 + p], half[:, 0:1], ALU.pow).then_inc(S["r_rstd"], 1)

            pool.sem_inc(S["ey_free"], 1)
            pool.wait_ge(S["best_out"], 2)
            pool.wait_ge(S["h_out"], 16 * TT)

            def gather(e):
                pool.tensor_copy(tokg[:, :], tokT[:, bass.ds(e, 1)]).then_inc(S["tokg_done"], 1)
                if isinstance(e, int):
                    pool.wait_ge(S["tokg_done"], e + 1)
                else:
                    past(S["tokg_done"], e + 1)
                pool.indirect_dma_start(out=xg[:, :], out_offset=None, in_=t["h2"],
                                        in_offset=bass.IndirectOffsetOnAxis(ap=tokg[:, 0:1], axis=0)).then_inc(S["gathered"], 16)

            def add_outputs(e):
                past(S["y_out"], 4 * e + 8)
                pool.indirect_dma_start(out=t["x1"], out_offset=bass.IndirectOffsetOnAxis(ap=toks[:, 0:1], axis=0),
                                        in_=ey[:, :], in_offset=None, compute_op=ALU.add).then_inc(S["scattered"], 16)
                past(S["scattered"], 16 * e + 16)
                pool.sem_inc(S["ey_free"], 1)

            def columns(e):
                pool.tensor_copy(toks[:, :], tokT[:, bass.ds(e, 1)]).then_inc(S["toks_done"], 1)
                pool.tensor_copy(gcol[:, :], gateT[:, bass.ds(e, 1)]).then_inc(S["gcol_done"], 1)
                past(S["toks_done"], e + 1)

            gather(0)
            with pool.Fori(0, NE - 1) as e:
                past(S["xtr"], 4 * e + 4)
                past(S["gathered"], 16 * e + 16)
                gather(e + 1)
                columns(e)
                add_outputs(e)
            columns(NE - 1)
            add_outputs(NE - 1)

            with pool.Fori(TT // 2, TT) as i:
                for p in range(2):
                    pool.wait_ge(S["r_mean"], 2 * i + (p + 1))
                    pool.tensor_tensor(rstd[:, p:p + 1], rsmall[:, 2 + p:3 + p], half[:, 0:1], ALU.pow).then_inc(S["r_rstd"], 1)

        @block.scalar
        def _(act):
            step = Steps(act, S["act_step"])

            def high(b, m):
                act.wait_ge(rawsem[m % RING], 32 * b + 16 * (m // RING + 1))
                if not (isinstance(b, int) and b == 0 and m < 4):
                    chunk_free(act, b, m)
                act.activation(whi[:, m % RING, :], raw[:, m % RING, :], ACT.Copy).then_inc(S["w_hi"], 1)

            def evict_rows(b):
                for n in range(8):
                    act.wait_ge(S["bank_ready"], 8 * b + (n + 1))
                    if not (isinstance(b, int) and b == 0 and n < 4):
                        act.wait_ge(S["stage_free"], 8 * b + (n - 3))
                    act.activation(stage[:, n % 4, :], ps[:, n, :], ACT.Copy, scale=rstd[:, n:n + 1])\
                        .then_inc(S["bank_staged"], 1)

            act.wait_ge(S["const_in"], 80)
            act.activation(wg[:, :, 0:16], wg_raw[:, :, :], ACT.Copy).then_inc(S["wg_hi"], 1)
            for k in range(KD):
                if k % 2 == 0 :
                    high(0, k // 2)
                act.wait_ge(xtsem[k % 2], 16 * (k // 2 + 1))
                act.activation(a_hi[:, k, :], (t0, t1)[k % 2][:, :], ACT.Copy, scale=gmix[:, k:k + 1]).then_inc(S["hT_hi"], 1)
                act.wait_ge(S["xnat"], 16 * (k + 1))
                act.activation(t2[:, 0:1024], t2[:, 0:1024], ACT.Square, accum_out=ssum[:, k:k + 1]).then_inc(S["xn_sq"], 1)
            for m in range(3):
                high(1, m)
            act.wait_ge(S["rstd_done"], 1)
            evict_rows(0)
            with act.Fori(1, ROWBLK) as b:
                for m in range(3, CPB):
                    high(b, m)
                for m in range(3):
                    high(b + 1, m)
                evict_rows(b)

            act.wait_ge(S["gates_ready"], 1)
            act.activation(g_two[:, :, :].rearrange("p t c -> p (t c)"), ps[:, 0, 0:TT * 32], ACT.Copy).then_inc(S["gates_copied"], 1)
            act.wait_ge(S["grows_ready"], 1)
            act.activation(t0[0:64, :], ps[0:64, 1:3, :].rearrange("p a b -> p (a b)"), ACT.Copy).then_inc(S["grows_out"], 1)
            act.activation(t1[0:64, :], ps[64:128, 1:3, :].rearrange("p a b -> p (a b)"), ACT.Copy).then_inc(S["grows_out"], 1)
            act.wait_ge(S["gate_arg"], 1)
            act.activation(t2[0:64, 0:1024], t2[0:64, 0:1024], ACT.Exp, scale=-1.0).then_inc(S["act_step"], 1)
            step.settle()
            act.activation(t2[0:64, 0:1024], t2[0:64, 0:1024], ACT.Ln, bias=1.0).then_inc(S["gate_act"], 1)
            act.wait_ge(S["gate_arg"], 2)
            act.activation(decay[:, :], decay[:, :], ACT.Exp).then_inc(S["gate_act"], 1)
            act.wait_ge(S["gate_arg"], 3)
            act.activation(t1[64:128, :], t3[0:64, :], ACT.Exp, scale=-1.0).then_inc(S["gate_act"], 1)
            act.wait_ge(S["gate_arg"], 4)
            act.activation(t0[64:128, :], t3[0:64, :], ACT.Exp).then_inc(S["gate_act"], 1)
            act.wait_ge(S["gate_arg"], 5)
            act.activation(t1[0:64, :], t3[0:64, :], ACT.Exp).then_inc(S["gate_act"], 1)

            with act.Fori(ROWBLK, ROWBLK + 2) as b:
                for m in range(3, CPB):
                    high(b, m)
                for m in range(3):
                    high(b + 1, m)
            with act.Fori(ROWBLK + 2, BLK) as b:
                for m in range(3, CPB):
                    high(b, m)
                    if m in (5, 7):
                        q = (m - 5) // 2
                        act.wait_ge(S["conv_free"], 2 * b + (q - 2 * (ROWBLK + 2) + 2))
                        act.activation(t0[:, :], t0[:, :], ACT.Silu, bias=cw[:, q, CONVW:CONVW + 1]).then_inc(S["silu_done"], 1)
                for m in range(3):
                    high(b + 1, m)

            act.sem_inc(S["pt_evicted"], 1)

            def expo(i, u):
                act.wait_ge(S["na_max"], 16 * i + (u + 1))
                w = WIDE[u % 8]
                act.activation(prob[:, u % 2, 0:w], prob[:, u % 2, 0:w], ACT.Exp, bias=ntop[:, u % 2:u % 2 + 1],
                               accum_out=psumr[:, u % 2:u % 2 + 1]).then_inc(S["exp_done"], 1)

            def evict_pt(i, u):
                act.wait_ge(S["transposed"], 16 * i + (u + 3))
                act.wait_ge(S["pv_done"], 16 * i + (u + 1))
                full = act.activation(flat2(probT[:, u % 2, 0:4, :]), PTP[:, 0:4 * P], ACT.Copy)
                if WIDE[u % 8] > 4 * P:
                    full = act.activation(probT[0:GW, u % 2, 4, :], PTP[0:GW, 4 * P:5 * P], ACT.Copy)
                full.then_inc(S["pt_evicted"], 1)

            def na_pair(i, last):
                for u in range(16):
                    if not (last and u == 15):
                        expo(i, u + 1)
                    evict_pt(i, u)

            expo(0, 0)
            with act.Fori(0, NAH // 2 - 1) as i:
                na_pair(i, False)
            na_pair(NAH // 2 - 1, True)

            act.sem_inc(S["st_out"], 1)
            act.sem_inc(S["t_done"], 2)
            with act.Fori(0, MLH // 2) as i:
                for hb in range(2):
                    h = 2 * i + hb
                    act.wait_ge(mlsem[hb], 80 * i + 80)
                    act.wait_ge(S["hcols_ready"], 2 * h + 2)

                    def weight(u):
                        n, d = ml_unit(u)
                        act.wait_ge(S["qkw_done"], 16 * h + (u + 1))
                        act.activation(wexp[:, u % 2, :], mbc[:, hb, d, n * P:(n + 1) * P], ACT.Exp, scale=-1.0,
                                       bias=hcols[:, hb, n, 0, d:d + 1]).then_inc(S["wexp_done"], 1)

                    weight(0)
                    act.wait_ge(S["st_ready"], h + 1)
                    for j in range(2):
                        act.wait_ge(S["qkw_done"], 16 * h + 2)
                        act.activation(st[:, j * BW:(j + 1) * BW], ps[:, j, :], ACT.Copy).then_inc(S["st_out"], 1)
                    for u in range(16):
                        n, d = ml_unit(u)
                        if u < 15:
                            weight(u + 1)
                        act.wait_ge(S["intr_done"], 16 * h + (u + 1))
                        act.wait_ge(S["hs_done"], 16 * h + (u + 1))
                        act.activation(inter[:, u % 2, :], ps[:, 6 + u % 2, 0:DV + 1], ACT.Copy,
                                       scale=hcols[:, hb, n, 2, d:d + 1]).then_inc(S["t_done"], 1)

            act.wait_ge(S["mh_free"], 2 + MLH)
            act.wait_ge(S["na_saved"], 16)
            act.wait_ge(S["hs_done"], 64 + 2)

            def stats(i, p):
                act.wait_ge(xasem[p], 48 * i + 48)
                if not (isinstance(i, int) and i == 0 and p == 0):
                    act.wait_ge(S["asm_stats"], 2 * i + p)
                act.activation(flat2(ps[:, 4:6, :]), mixA[p], ACT.Square, accum_out=msq[:, p, 0:1])
                for h in range(MLH):
                    act.activation(ps[:, 6 + h // 2, (h % 2) * DV:(h % 2 + 1) * DV], mixB[p][:, h * DV:(h + 1) * DV],
                                   ACT.Square, accum_out=msq[:, p, 1 + h:2 + h])
                act.activation(mixO[p], mixO[p], ACT.Sigmoid).then_inc(S["asm_stats"], 1)

            def mix_high(i, p):
                T = 2 * i + p
                for g in range(4):
                    act.wait_ge(S["asm_tr"], 4 * T + (g + 1))
                    for j in range(4):
                        k = 4 * g + j
                        gain = nag[:, k:k + 1] if k < NAH else mlg[:, k - NAH:k - NAH + 1]
                        act.activation(a_hi[:, k, bass.ds(T * P, P)], ps[:, g, j * P:(j + 1) * P], ACT.Copy, scale=gain)\
                            .then_inc(S["mixT_hi"], 1)

            def mix_pair(i, last):
                stats(i, 1)
                mix_high(i, 0)
                if not last:
                    stats(i + 1, 0)
                mix_high(i, 1)

            stats(0, 0)
            with act.Fori(0, TT // 2 - 1) as i:
                mix_pair(i, False)
            mix_pair(TT // 2 - 1, True)

            def evict_plain(b):
                for n in range(8):
                    act.wait_ge(S["bank_ready"], 8 * b + (n + 1))
                    act.wait_ge(S["stage_free"], 8 * b + (n - 3))
                    act.activation(stage[:, n % 4, :], ps[:, n, :], ACT.Copy).then_inc(S["bank_staged"], 1)

            with act.Fori(BLK, BLK + OBLK - 1) as b:
                for m in range(3, CPB):
                    high(b, m)
                for m in range(3):
                    high(b + 1, m)
                evict_plain(b)
            for m in range(3, CPB):
                high(BLK + OBLK - 1, m)
            evict_plain(BLK + OBLK - 1)

            def r_square(i, p):
                act.wait_ge(rxsem[p], 16 * i + 16)
                act.wait_ge(S["rh_free"], 2 * i + (p + 1))
                act.wait_ge(S["r_tr"], 8 * i + (4 * p + 4))
                act.activation(rh[:, p, :], rx[:, p, :], ACT.Square, accum_out=rsmall[:, p:p + 1]).then_inc(S["r_sq"], 1)

            def r_evict(i, p):
                T = 2 * i + p
                act.wait_ge(S["r_logit"], T + 1)
                for g in range(2):
                    act.wait_ge(S["r_tr"], 4 * T + (g + 8 + 1))
                    act.activation(flat2(rT[:, 4 * g:4 * g + 4, :]), ps[:, g, :], ACT.Copy).then_inc(S["r_tA"], 1)

            def r_pair(i, last):
                r_square(i, 1)
                r_evict(i, 0)
                if not last:
                    r_square(i + 1, 0)
                r_evict(i, 1)

            r_square(0, 0)
            with act.Fori(0, TT // 2 - 1) as i:
                r_pair(i, False)
            r_pair(TT // 2 - 1, True)
            act.wait_ge(S["smax"], 2)
            act.activation(affs[:, :, :], affs[:, :, :], ACT.Exp).then_inc(S["r_exp"], 1)
            for a in range(2):
                act.wait_ge(S["aff_tr"], a + 1)
                act.activation(affT[:, a * BW:(a + 1) * BW], ps[0:NE, a, :], ACT.Copy).then_inc(S["aff_out"], 1)

            def piece_high(e, j):
                act.wait_ge(ersem[j % ERAW], 16 * (EPC // ERAW) * e + (16 * (j // ERAW + 1) + ER0[j % ERAW]))
                if j >= ESPL:
                    act.wait_ge(*used(e, j - ESPL))
                elif not (isinstance(e, int) and e == 0):
                    act.wait_ge(*used(e - 1, j + EPC - ESPL))
                act.activation(ehi[:, j % ESPL, :], eraw[:, j % ERAW, :], ACT.Copy).then_inc(S["e_hi"], 1)

            def x_high(e, g):
                act.wait_ge(S["xtr"], 4 * e + (g + 1))
                act.activation(flat2(xh[:, 4 * g:4 * g + 4, :]), ps[:, 6 + g % 2, :], ACT.Copy).then_inc(S["x_hi"], 1)

            def h_high(e, g):
                act.wait_ge(S["htr"], 2 * e + (g + 1))
                act.activation(flat2(hh[:, 4 * g:4 * g + 4, :]), ps[:, 4 + g, :], ACT.Copy).then_inc(S["h_hi"], 1)

            def expert(e, last):
                for j in range(ESPL, 38):
                    piece_high(e, j)
                act.wait_ge(S["gu_ready"], e + 1)
                for c in range(2):
                    act.activation(hact[:, c * BW:(c + 1) * BW], ps[:, c, :], ACT.Silu).then_inc(S["silu2"], 1)
                if last:
                    h_high(e, 0)
                    h_high(e, 1)
                else:
                    x_high(e + 1, 0)
                    x_high(e + 1, 1)
                    h_high(e, 0)
                    h_high(e, 1)
                    x_high(e + 1, 2)
                    x_high(e + 1, 3)
                for j in range(38, EPC):
                    piece_high(e, j)
                if not last:
                    for j in range(ESPL):
                        piece_high(e + 1, j)
                act.wait_ge(S["gcol_done"], e + 1)
                act.wait_ge(S["ey_free"], e + 1)
                for c in range(2):
                    act.wait_ge(S["y_ready"], 4 * e + (c + 1))
                    act.activation(ey[:, c * BW:(c + 1) * BW], ps[:, 4 + c, :], ACT.Copy, scale=gcol[:, 0:1]).then_inc(S["y_out"], 1)

            for j in range(ESPL):
                piece_high(0, j)
            for g in range(4):
                x_high(0, g)
            with act.Fori(0, NE - 1) as e:
                expert(e, False)
            expert(NE - 1, True)

            with act.Fori(TT // 2, TT) as i:
                for p in range(2):
                    act.wait_ge(rxsem[p], 16 * i + 16)
                    act.wait_ge(S["rh_free"], 2 * i + (p + 1))
                    act.activation(rh[:, p, :], rx[:, p, :], ACT.Square, accum_out=rsmall[:, p:p + 1]).then_inc(S["r_sq"], 1)

        @block.vector
        def _(dve):
            step = Steps(dve, S["dve_step"])

            def low(b, m):
                dve.wait_ge(S["w_hi"], CPB * b + (m + 1))
                dve.tensor_tensor(wlo[:, m % RING, :], raw[:, m % RING, :], whi[:, m % RING, :].bitcast(F32), ALU.subtract)\
                    .then_inc(S["w_lo"], 1)

            dve.wait_ge(S["const_in"], 80)
            dve.wait_ge(S["wg_hi"], 1)
            dve.tensor_tensor(wg[:, :, 16:32], wg_raw[:, :, :], wg[:, :, 0:16].bitcast(F32), ALU.subtract).then_inc(S["wg_done"], 1)
            for k in range(KD):
                if k % 2 == 0 :
                    low(0, k // 2)
                dve.wait_ge(S["hT_hi"], k + 1)
                dve.scalar_tensor_tensor(out=a_lo[:, k, :], in0=(t0, t1)[k % 2][:, :], scalar=gmix[:, k:k + 1],
                                         in1=a_hi[:, k, :].bitcast(F32), op0=ALU.mult, op1=ALU.subtract).then_inc(S["hT_lo"], 1)
            for m in range(3):
                low(1, m)
            dve.wait_ge(S["xn_sq"], KD)
            ss = ssum[:, :].rearrange("p (t h) -> p t h", h=2)
            dve.tensor_tensor(meansq[:, :], ss[:, :, 0], ss[:, :, 1], ALU.add).then_inc(S["dve_step"], 1)
            step.settle()
            dve.tensor_scalar(meansq[:, :], meansq[:, :], 1.0 / D, EPS, ALU.mult, ALU.add).then_inc(S["meansq_done"], 1)
            with dve.Fori(1, ROWBLK) as b:
                for m in range(3, CPB):
                    low(b, m)
                for m in range(3):
                    low(b + 1, m)

            def bc(ap, n):
                return ap.unsqueeze(2).broadcast_to([ap.shape[0], ap.shape[1], n])

            dve.wait_ge(S["gates_copied"], 1)
            dve.tensor_tensor(g_nat[:, :, :], g_two[:, :, 0:16], g_two[:, :, 16:32], ALU.add).then_inc(S["dve_step"], 1)
            step.settle()
            dve.wait_ge(S["rstd_done"], 1)
            dve.tensor_tensor(g_nat[:, :, :], g_nat[:, :, :], bc(rstd[:, :], 16), ALU.mult).then_inc(S["dve_step"], 1)
            step.settle()
            dve.wait_ge(S["gpad_zero"], 5)
            gpad = t2[:, 0:1024].rearrange("p (t c) -> p t c", c=P)
            for q, at in enumerate((0, 64, 32, 96)):
                dve.tensor_tensor(gpad[:, :, at:at + 4], g_nat[:, :, 4 * q:4 * q + 4],
                                  g_bias[:, 4 * q:4 * q + 4].unsqueeze(1).broadcast_to([P, TT, 4]), ALU.add)\
                    .then_inc(S["gpad_done"], 1)
            T0, T1, T2, T3 = t0[0:64, :], t1[0:64, :], t2[0:64, 0:1024], t3[0:64, :]
            dve.wait_ge(S["grows_out"], 2)
            dve.scalar_tensor_tensor(out=T2, in0=T1, scalar=-1.0, in1=T1, op0=ALU.mult, op1=ALU.max).then_inc(S["gate_arg"], 1)
            dve.wait_ge(S["gate_act"], 1)
            dve.scalar_tensor_tensor(out=T1, in0=T1, scalar=0.0, in1=T2, op0=ALU.min, op1=ALU.subtract).then_inc(S["dve_step"], 1)
            step.settle()
            dve.wait_ge(S["mask_done"], 1)
            ways = ((slice(0, 4), 1), (slice(32, 36), -1))
            for r, way in ways:
                dve.tensor_tensor_scan(out=t1[r, ::way], data0=t3[r, :], data1=t1[r, ::way], initial=0.0,
                                       op0=ALU.mult, op1=ALU.add).then_inc(S["dve_step"], 1)
                step.settle()
            dve.tensor_tensor(T0, T0, T1, ALU.subtract).then_inc(S["dve_step"], 1)
            step.settle()
            dve.tensor_scalar(T3, T3, -1.0, -NEG, ALU.add, ALU.mult).then_inc(S["dve_step"], 1)
            step.settle()
            for r, way in ways:
                dve.tensor_tensor_scan(out=t2[r, 0:1024][:, ::way], data0=t3[r, :], data1=t0[r, ::way], initial=0.0,
                                       op0=ALU.add, op1=ALU.max).then_inc(S["dve_step"], 1)
                step.settle()
            T1n, T2n = T1.rearrange("p (n j) -> p n j", j=P), T2.rearrange("p (n j) -> p n j", j=P)
            T0n, T3n = T0.rearrange("p (n j) -> p n j", j=P), T3.rearrange("p (n j) -> p n j", j=P)
            for r, way in ways:
                e = P - 1 if way > 0 else 0
                dve.tensor_copy(b_last[r, :], T1n[r, :, e]).then_inc(S["dve_step"], 1)
                step.settle()
                dve.tensor_copy(c_last[r, :], T2n[r, :, e]).then_inc(S["dve_step"], 1)
                step.settle()
            for r, way in ways:
                dve.tensor_tensor_scan(out=m_next[r, 1:TT + 1][:, ::way], data0=c_last[r, ::way], data1=b_last[r, ::way],
                                       initial=0.0, op0=ALU.max, op1=ALU.add).then_inc(S["dve_step"], 1)
                step.settle()
                at = 0 if way > 0 else 2
                dve.tensor_copy(m_prev[r, :], m_next[r, at:at + TT]).then_inc(S["dve_step"], 1)
                step.settle()
            dve.tensor_tensor(m_end[:, :], m_prev[:, :], c_last[:, :], ALU.max).then_inc(S["dve_step"], 1)
            step.settle()
            dve.tensor_tensor(decay[:, :], m_prev[:, :], m_end[:, :], ALU.subtract).then_inc(S["gate_arg"], 1)
            dve.tensor_tensor(T2n, T2n, bc(m_prev[:, :], P), ALU.max).then_inc(S["dve_step"], 1)
            step.settle()
            dve.tensor_tensor(T3, T1, T2, ALU.add).then_inc(S["gate_arg"], 1)
            dve.tensor_scalar(T0, T0, LNS, None, ALU.add).then_inc(S["dve_step"], 1)
            step.settle()
            dve.wait_ge(S["gate_act"], 3)
            dve.tensor_tensor(T3n, T0n, bc(m_end[:, :], P), ALU.subtract).then_inc(S["gate_arg"], 1)
            dve.wait_ge(S["gate_act"], 4)
            dve.tensor_tensor(T3n, bc(m_prev[:, :], P), T2n, ALU.subtract).then_inc(S["gate_arg"], 1)
            dve.wait_ge(S["acc_free"], 1)
            dve.memset(t2[:, 0:2], 0.0).then_inc(S["dve_step"], 1)
            step.settle()
            dve.memset(t2[:, 1026:1028], 0.0).then_inc(S["conv_free"], 1)

            def evict_feats(b):
                for n in range(8):
                    dve.wait_ge(S["bank_ready"], 8 * b + (n + 1))
                    dve.wait_ge(S["stage_free"], 8 * b + (n - 3))
                    dve.tensor_tensor(stage[:, n % 4, :], ps[:, n, :], rstd_bc[:, (n % 2) * BW:(n % 2 + 1) * BW], ALU.mult)\
                        .then_inc(S["bank_staged"], 1)

            dve.wait_ge(S["rstd_bc_in"], 16)
            dve.wait_ge(S["gate_act"], 5)
            with dve.Fori(ROWBLK, ROWBLK + 2) as b:
                for m in range(3, CPB):
                    low(b, m)
                for m in range(3):
                    low(b + 1, m)
                evict_feats(b)
            with dve.Fori(ROWBLK + 2, BLK) as b:
                step.enter(b - (ROWBLK + 2), 2 * (CONVW - 1))
                for m in range(3, CPB):
                    low(b, m)
                    if m in (4, 6):
                        q = (m - 4) // 2
                        c = 2 * b + (q - 2 * (ROWBLK + 2))
                        dve.wait_ge(S["conv_in"], 32 * c + 32)
                        dve.wait_ge(S["acc_free"], c + 1)
                        dve.tensor_scalar(t0[:, :], t2[:, 0:1024], cw[:, q, 0:1], None, ALU.mult).then_inc(S["dve_step"], 1)
                        step.settle()
                        for j in range(1, CONVW):
                            last = dve.scalar_tensor_tensor(out=t0[:, :], in0=t2[:, j:j + 1024], scalar=cw[:, q, j:j + 1],
                                                            in1=t0[:, :], op0=ALU.mult, op1=ALU.add)
                            if j < CONVW - 1:
                                last.then_inc(S["dve_step"], 1)
                                step.settle()
                            else:
                                last.then_inc(S["conv_free"], 1)
                for m in range(3):
                    low(b + 1, m)
                evict_feats(b)
                step.leave(BLK - ROWBLK - 2)

            dve.wait_ge(S["cols_ready"], 1)
            for q in range(4):
                src = ps[:, 2 * (q // 2):2 * (q // 2) + 2, :].rearrange("p a (n r) -> p (a n) r", r=P)
                src = src[:, :, 64 * (q % 2):64 * (q % 2) + 64].rearrange("p n (d h) -> p n d h", d=2)[:, :, :, 0:MLH]
                dve.tensor_copy(cols[:, :, q, :, :], src).then_inc(S["cols_out"], 1)

            dve.sem_inc(S["scored"], 2)
            dve.sem_inc(S["na_out_done"], 2)

            def score(i, u):
                hb, p, w = u // 8, u % 8, WIDE[u % 8]
                if u % 8 == 0:
                    dve.wait_ge(S["bias_ready"], 4 * i + (2 * hb + 2))
                dve.wait_ge(S["qk_done"], 16 * i + (u + 1))
                dve.wait_ge(S["transposed"], 16 * i + (u + 1))
                dve.sem_inc(S["dve_past"], 1)
                b = flat2(bias9[:, hb, :, :]) if w > 8 * GW else flat2(bias[:, hb, BROW[p] - 1:BROW[p] + 7, :])
                dve.tensor_tensor_reduce(out=prob[:, u % 2, 0:w], in0=SC[u % 2][:, 0:w], in1=b, scale=1.0, scalar=3 * NEG,
                                         op0=ALU.add, op1=ALU.max, accum_out=top[:, u % 2:u % 2 + 1]).then_inc(S["scored"], 1)
                dve.wait_ge(S["scored"], 16 * i + (u + 3))
                dve.tensor_scalar(ntop[:, u % 2:u % 2 + 1], top[:, u % 2:u % 2 + 1], -1.0, None, ALU.mult).then_inc(S["na_max"], 1)

            def finish(i, u):
                dve.wait_ge(S["exp_done"], 16 * i + (u + 1))
                dve.reciprocal(pinv[:, u % 2:u % 2 + 1], psumr[:, u % 2:u % 2 + 1]).then_inc(S["na_step"], 1)
                dve.wait_ge(S["na_step"], 16 * i + (u + 1))
                dve.wait_ge(S["pv_done"], 16 * i + (u + 3))
                dve.tensor_scalar(na_out[:, u % 8, bass.ds((2 * i + u // 8) * HD, HD)], ps[:, 6 + u % 2, 0:HD],
                                  pinv[:, u % 2:u % 2 + 1], None, ALU.mult).then_inc(S["na_out_done"], 1)

            def na_pair(i, last):
                for u in range(16):
                    if not (last and u == 15):
                        score(i, u + 1) if u < 15 else score(i + 1, 0)
                    finish(i, u)

            score(0, 0)
            with dve.Fori(0, NAH // 2 - 1) as i:
                na_pair(i, False)
            na_pair(NAH // 2 - 1, True)

            dve.wait_ge(S["gates_in"], 32)
            dve.sem_inc(S["qkw_done"], 2)
            dve.sem_inc(S["c_updated"], 2)
            dve.sem_inc(S["hs_done"], 2)
            with dve.Fori(0, MLH // 2) as i:
                step.enter(i, 2 * 16 * 4)
                for hb in range(2):
                    h = 2 * i + hb
                    dve.wait_ge(S["c_updated"], 16 * h + 2)
                    dve.wait_ge(S["cols_out"], 4)
                    dve.memset(cst[:, :, :], 0.0).then_inc(S["c_zeroed"], 1)
                    dve.tensor_copy(hcols[:, hb, :, :, :],
                                    cols[:, :, :, :, bass.ds(h, 1)].rearrange("p n q d h -> p n q (d h)")).then_inc(S["hcols_ready"], 1)
                    dve.tensor_copy(hdec[:, hb, :, :],
                                    decbc[:, :, bass.ds(h, 1), :].rearrange("p d h n -> p (d h) n")).then_inc(S["hcols_ready"], 1)
                    dve.wait_ge(S["kn_ready"], h + 1)
                    dve.wait_ge(S["kw_done"], 16 * h + 1)
                    for j in range(2):
                        dve.tensor_copy(flat2(kn[:, 4 * j:4 * j + 4, :]), ps[:, j, :]).then_inc(S["kn_out"], 1)
                    dve.wait_ge(S["mh_free"], h + 1)

                    def weigh(u):
                        n, d = ml_unit(u)
                        dve.wait_ge(S["masked"], 16 * h + (u + 1))
                        dve.wait_ge(S["num_done"], 16 * h + (u + 1))
                        dve.tensor_tensor(qkw[:, u % 2, :], st[:, n * P:(n + 1) * P], wexp[:, u % 2, :], ALU.mult)\
                            .then_inc(S["qkw_done"], 1)

                    dve.wait_ge(S["st_out"], 2 * h + 3)
                    weigh(0)
                    dve.wait_ge(S["hcols_ready"], 2 * h + 2)
                    for u in range(16):
                        n, d = ml_unit(u)
                        if u < 15:
                            weigh(u + 1)
                        if u < 2:
                            dve.wait_ge(S["c_zeroed"], h + 1)
                        else:
                            dve.wait_ge(S["c_updated"], 16 * h + (u + 1))
                        dve.wait_ge(S["kv_done"], 16 * h + (u + 3))
                        dve.wait_ge(S["intr_done"], 16 * h + (u + 1))
                        dve.scalar_tensor_tensor(out=cst[:, d, :], in0=cst[:, d, :], scalar=hdec[:, hb, d, n:n + 1],
                                                 in1=ps[:, 2 + u % 2, 0:DV + 1], op0=ALU.mult, op1=ALU.add).then_inc(S["c_updated"], 1)
                        dve.wait_ge(S["num_done"], 16 * h + (u + 3))
                        dve.wait_ge(S["t_done"], 16 * h + (u + 3))
                        dve.tensor_tensor(hsum[:, u % 2, :], ps[:, 4 + u % 2, 0:DV + 1], inter[:, u % 2, :], ALU.add)\
                            .then_inc(S["hs_done"], 1)
                        dve.wait_ge(S["hs_done"], 16 * h + (u + 3))
                        s1, dn = hsum[:, u % 2, DV:DV + 1], den[:, u % 2:u % 2 + 1]
                        dve.scalar_tensor_tensor(out=dn, in0=s1, scalar=-1.0, in1=s1, op0=ALU.mult, op1=ALU.max).then_inc(S["dve_step"], 1)
                        step.settle()
                        dve.tensor_scalar(dn, dn, hcols[:, hb, n, 3, d:d + 1], None, ALU.max).then_inc(S["dve_step"], 1)
                        step.settle()
                        dve.reciprocal(dn, dn).then_inc(S["dve_step"], 1)
                        step.settle()
                        if u < 8:
                            last = dve.tensor_scalar(mh[:, hb, n, :], hsum[:, u % 2, 0:DV], dn, None, ALU.mult)
                        else:
                            last = dve.scalar_tensor_tensor(out=mh[:, hb, n, :], in0=hsum[:, u % 2, 0:DV], scalar=dn,
                                                            in1=mh[:, hb, n, :], op0=ALU.mult, op1=ALU.add)
                        last.then_inc(S["dve_step"], 1)
                        step.settle()
                    dve.sem_inc(S["ml_head_done"], 1)
                step.leave(MLH // 2)

            dve.wait_ge(S["mh_free"], 2 + MLH)
            dve.sem_inc(S["mixT_lo"], KD)

            def scale_mix(i, p):
                T = 2 * i + p
                dve.wait_ge(S["asm_stats"], T + 1)
                dve.tensor_scalar(msq[:, p, 0:1], msq[:, p, 0:1], 1.0 / (NAH * HD), EPS, ALU.mult, ALU.add)
                dve.tensor_scalar(msq[:, p, 1:5], msq[:, p, 1:5], 1.0 / DV, EPS, ALU.mult, ALU.add).then_inc(S["asm_mean"], 1)
                dve.wait_ge(S["rs_done"], T + 1)
                dve.tensor_scalar(mixA[p], mixA[p], rs[:, p, 0:1], None, ALU.mult)
                for h in range(MLH):
                    at = slice(h * DV, (h + 1) * DV)
                    last = dve.scalar_tensor_tensor(out=mixB[p][:, at], in0=mixB[p][:, at], scalar=rs[:, p, 1 + h:2 + h],
                                                    in1=mixO[p][:, at], op0=ALU.mult, op1=ALU.mult)
                last.then_inc(S["asm_scaled"], 1)

            def mix_low(i, p):
                T = 2 * i + p
                for g in range(4):
                    dve.wait_ge(S["mixT_hi"], 16 * T + (4 * g + 4))
                    for j in range(4):
                        k = 4 * g + j
                        gain = nag[:, k:k + 1] if k < NAH else mlg[:, k - NAH:k - NAH + 1]
                        dve.scalar_tensor_tensor(out=a_lo[:, k, bass.ds(T * P, P)], in0=ps[:, g, j * P:(j + 1) * P], scalar=gain,
                                                 in1=a_hi[:, k, bass.ds(T * P, P)].bitcast(F32), op0=ALU.mult,
                                                 op1=ALU.subtract).then_inc(S["mixT_lo"], 1)

            def mix_pair(i, last):
                scale_mix(i, 1)
                mix_low(i, 0)
                if not last:
                    scale_mix(i + 1, 0)
                mix_low(i, 1)

            scale_mix(0, 0)
            with dve.Fori(0, TT // 2 - 1) as i:
                mix_pair(i, False)
            mix_pair(TT // 2 - 1, True)

            with dve.Fori(BLK, BLK + OBLK - 1) as b:
                for m in range(3, CPB):
                    low(b, m)
                for m in range(3):
                    low(b + 1, m)
            for m in range(3, CPB):
                low(BLK + OBLK - 1, m)

            dve.wait_ge(S["rc_in"], 32)

            def r_normal(i, p):
                dve.wait_ge(S["r_sq"], 2 * i + (p + 1))
                dve.tensor_scalar(rsmall[:, 2 + p:3 + p], rsmall[:, p:p + 1], 1.0 / D, EPS, ALU.mult, ALU.add).then_inc(S["r_mean"], 1)
                dve.wait_ge(S["r_rstd"], 2 * i + (p + 1))
                dve.scalar_tensor_tensor(out=rh[:, p, :], in0=rx[:, p, :], scalar=rstd[:, p:p + 1], in1=gbc[:, :],
                                         op0=ALU.mult, op1=ALU.mult).then_inc(S["r_norm"], 1)

            def r_evict(i, p):
                T = 2 * i + p
                dve.wait_ge(S["r_logit"], T + 1)
                for g in range(2, 4):
                    dve.wait_ge(S["r_tr"], 4 * T + (g + 8 + 1))
                    dve.tensor_copy(flat2(rT[:, 4 * g:4 * g + 4, :]), ps[:, g, :]).then_inc(S["r_tD"], 1)

            def r_pair(i, last):
                r_normal(i, 1)
                r_evict(i, 0)
                if not last:
                    r_normal(i + 1, 0)
                r_evict(i, 1)

            r_normal(0, 0)
            with dve.Fori(0, TT // 2 - 1) as i:
                r_pair(i, False)
            r_pair(TT // 2 - 1, True)
            lg = ps[:, 4, 0:TT * NE].rearrange("p (t e) -> p t e", e=NE)
            dve.wait_ge(S["r_logit"], TT + 1)
            dve.tensor_reduce(out=smx[:, :], in_=lg, axis=AX.X, op=ALU.max).then_inc(S["smax"], 1)
            dve.wait_ge(S["smax"], 1)
            dve.tensor_tensor(affs[:, :, :], lg, bc(smx[:, :], NE), ALU.subtract).then_inc(S["smax"], 1)
            dve.wait_ge(S["r_exp"], 1)
            dve.tensor_reduce(out=smx[:, :], in_=affs[:, :, :], axis=AX.X, op=ALU.add).then_inc(S["dve_step"], 1)
            step.settle()
            dve.reciprocal(smx[:, :], smx[:, :]).then_inc(S["dve_step"], 1)
            step.settle()
            dve.tensor_tensor(affs[:, :, :], affs[:, :, :], bc(smx[:, :], NE), ALU.mult).then_inc(S["affn"], 1)
            dve.wait_ge(S["aff_out"], 2)
            for r in range(TOPR):
                at = slice(8 * r, 8 * r + 8)
                dve.max(best[:, at], affT[:, :]).then_inc(S["dve_step"], 1)
                step.settle()
                dve.max_index(besti[:, at], best[:, at], affT[:, :]).then_inc(S["dve_step"], 1)
                step.settle()
                if r < TOPR - 1:
                    dve.match_replace(out=affT[:, :], in_to_replace=best[:, at], in_values=affT[:, :], imm_value=-1.0)\
                        .then_inc(S["dve_step"], 1)
                    step.settle()
            dve.tensor_copy(bestf[:, :], besti[:, :]).then_inc(S["affn"], 1)
            dve.wait_ge(S["aff_tr"], 3)
            dve.tensor_copy(gateT[:, :], ps[:, 0, 0:NE]).then_inc(S["best_out"], 1)
            dve.tensor_copy(tokT[:, :], ps[:, 0, NE:2 * NE]).then_inc(S["best_out"], 1)

            def piece_low(e, j):
                dve.wait_ge(S["e_hi"], EPC * e + (j + 1))
                dve.tensor_tensor(elo[:, j % ESPL, :], eraw[:, j % ERAW, :], ehi[:, j % ESPL, :].bitcast(F32), ALU.subtract)\
                    .then_inc(S["e_lo"], 1)

            def x_low(e, g):
                dve.wait_ge(S["x_hi"], 4 * e + (g + 1))
                dve.tensor_tensor(flat2(xl[:, 4 * g:4 * g + 4, :]), ps[:, 6 + g % 2, :],
                                  flat2(xh[:, 4 * g:4 * g + 4, :]).bitcast(F32), ALU.subtract).then_inc(S["x_lo"], 1)

            def h_low(e, g):
                dve.wait_ge(S["h_hi"], 2 * e + (g + 1))
                dve.tensor_tensor(flat2(hl[:, 4 * g:4 * g + 4, :]), ps[:, 4 + g, :],
                                  flat2(hh[:, 4 * g:4 * g + 4, :]).bitcast(F32), ALU.subtract).then_inc(S["h_lo"], 1)

            def expert(e, last):
                for j in range(ESPL, 38):
                    piece_low(e, j)
                for c in range(2):
                    dve.wait_ge(S["silu2"], 2 * e + (c + 1))
                    dve.tensor_tensor(hact[:, c * BW:(c + 1) * BW], ps[:, 2 + c, :], hact[:, c * BW:(c + 1) * BW], ALU.mult)\
                        .then_inc(S["hmul"], 1)
                if last:
                    h_low(e, 0)
                    h_low(e, 1)
                else:
                    x_low(e + 1, 0)
                    x_low(e + 1, 1)
                    h_low(e, 0)
                    h_low(e, 1)
                    x_low(e + 1, 2)
                    x_low(e + 1, 3)
                for j in range(38, EPC):
                    piece_low(e, j)
                if not last:
                    for j in range(ESPL):
                        piece_low(e + 1, j)
                dve.wait_ge(S["gcol_done"], e + 1)
                dve.wait_ge(S["ey_free"], e + 1)
                for c in range(2, 4):
                    dve.wait_ge(S["y_ready"], 4 * e + (c + 1))
                    dve.tensor_scalar(ey[:, c * BW:(c + 1) * BW], ps[:, 4 + c, :], gcol[:, 0:1], None, ALU.mult).then_inc(S["y_out"], 1)

            for j in range(ESPL):
                piece_low(0, j)
            for g in range(4):
                x_low(0, g)
            with dve.Fori(0, NE - 1) as e:
                expert(e, False)
            expert(NE - 1, True)

            dve.wait_ge(S["rc_in"], 48)
            with dve.Fori(TT // 2, TT) as i:
                for p in range(2):
                    r_normal(i, p)

        @block.tensor
        def _(pe):
            def rows_block(b, src_hi, src_lo, first=False, bank_wait=True):
                for k in range(KD):
                    m = k // 2
                    if k % 2 == 0:
                        pe.wait_ge(S["w_lo"], CPB * b + (m + 1))
                    if first:
                        pe.wait_ge(S["hT_lo"], k + 1)
                    hi = whi[:, m % RING, (k % 2) * BW:(k % 2 + 1) * BW]
                    lo = wlo[:, m % RING, (k % 2) * BW:(k % 2 + 1) * BW]
                    for n in range(TT):
                        if k == 0 and bank_wait:
                            pe.wait_ge(S["bank_staged"], 8 * b + (n - 7))
                        xs = src_hi[:, k, n * P:(n + 1) * P]
                        pe.matmul(ps[:, n, :], xs, hi, start=(k == 0), stop=False)
                        pe.matmul(ps[:, n, :], xs, lo, start=False, stop=False)
                        last = pe.matmul(ps[:, n, :], src_lo[:, k, n * P:(n + 1) * P], hi, start=False, stop=(k == KD - 1))
                        if k == KD - 1:
                            last.then_inc(S["bank_ready"], 1)
                    if k % 2 == 1 and k < KD - 1:
                        last.then_inc(S["w_used"], 1)

            def feats_block(b, bank_wait=True):
                for k in range(KD):
                    m = k // 2
                    if k % 2 == 0:
                        pe.wait_ge(S["w_lo"], CPB * b + (m + 1))
                    for g in range(4):
                        at = (k % 2) * BW + g * P
                        hi, lo = whi[:, m % RING, at:at + P], wlo[:, m % RING, at:at + P]
                        for w, src in ((hi, a_hi), (hi, a_lo), (lo, a_hi)):
                            for h in range(2):
                                n = 2 * g + h
                                if k == 0 and w is hi and src is a_hi and bank_wait:
                                    pe.wait_ge(S["bank_staged"], 8 * b + (n - 7))
                                last = pe.matmul(ps[:, n, :], w, src[:, k, h * BW:(h + 1) * BW],
                                                 start=(k == 0 and w is hi and src is a_hi),
                                                 stop=(k == KD - 1 and w is lo))
                                if k == KD - 1 and w is lo:
                                    last.then_inc(S["bank_ready"], 1)
                    if k % 2 == 1 and k < KD - 1:
                        last.then_inc(S["w_used"], 1)

            rows_block(0, a_hi, a_lo, first=True, bank_wait=False)
            with pe.Fori(1, ROWBLK) as b:
                rows_block(b, a_hi, a_lo)
            pe.wait_ge(S["bank_staged"], 8 * ROWBLK)
            pe.wait_ge(S["wg_done"], 1)
            for n in range(TT):
                for k in range(KD):
                    pe.matmul(ps[:, 0, n * 32:n * 32 + 32], a_hi[:, k, n * P:(n + 1) * P], wg[:, k, :], start=(k == 0), stop=False,
                              skip_group_check=True)
                    last = pe.matmul(ps[:, 0, n * 32:n * 32 + 16], a_lo[:, k, n * P:(n + 1) * P], wg[:, k, 0:16], start=False,
                                     stop=(k == KD - 1), skip_group_check=True)
            last.then_inc(S["gates_ready"], 1)
            pe.wait_ge(S["gpad_done"], 4)
            pe.wait_ge(S["ident_done"], 1)
            for n in range(TT):
                last = pe.transpose(ps[:, 1 + n // 4, (n % 4) * P:(n % 4 + 1) * P], t2[:, n * P:(n + 1) * P], ident[:, :])
            last.then_inc(S["grows_ready"], 1)
            pe.wait_ge(S["gates_copied"], 1)
            pe.wait_ge(S["grows_out"], 2)
            with pe.Fori(ROWBLK, BLK) as b:
                feats_block(b)

            pe.wait_ge(S["gates_in"], 32)
            pe.wait_ge(S["bank_staged"], 8 * BLK)
            for a in range(2):
                for n in range(TT):
                    last = pe.transpose(ps[:, 2 * a + n // 4, (n % 4) * P:(n % 4 + 1) * P], qrows[:, a, n * P:(n + 1) * P], ident[:, :])
            last.then_inc(S["cols_ready"], 1)
            pe.wait_ge(S["cols_out"], 4)

            pe.sem_inc(S["transposed"], 2)
            pe.sem_inc(S["pv_done"], 2)

            def qk(i, u):
                hb, p, w = u // 8, u % 8, WIDE[u % 8]
                if p == 0:
                    pe.wait_ge(S["q_scaled"], 2 * i + (hb + 1))
                    pe.wait_ge(nkvsem[hb], 32 * i + 32)
                pe.wait_ge(S["scored"], 16 * i + (u + 1))
                q, k0 = naq[:, hb, p * P:(p + 1) * P], KEY0[p] * P
                last = pe.matmul(SC[u % 2][:, 0:BW], q, nak[:, hb, k0:k0 + BW], start=True, stop=True)
                if w > BW:
                    last = pe.matmul(SC[u % 2][:, BW:w], q, nak[:, hb, k0 + BW:k0 + w], start=True, stop=True)
                last.then_inc(S["qk_done"], 1)

            def tr(i, u):
                pe.wait_ge(S["exp_done"], 16 * i + (u + 1))
                pe.wait_ge(S["pt_evicted"], 16 * i + (u + 1))
                for j in range(4):
                    last = pe.transpose(PTP[:, j * P:(j + 1) * P], prob[:, u % 2, j * P:(j + 1) * P], ident[:, :])
                if WIDE[u % 8] > 4 * P:
                    last = pe.transpose(PTP[0:GW, 4 * P:5 * P], prob[:, u % 2, 4 * P:4 * P + GW], ident[:, :])
                last.then_inc(S["transposed"], 1)

            def pv(i, u):
                hb, p = u // 8, u % 8
                pe.wait_ge(S["pt_evicted"], 16 * i + (u + 2))
                pe.wait_ge(S["na_out_done"], 16 * i + (u + 1))
                nk = 5 if WIDE[p] > 4 * P else 4
                for j in range(nk):
                    r = P if j < 4 else GW
                    last = pe.matmul(ps[:, 6 + u % 2, 0:HD], probT[0:r, u % 2, j, :], nav[0:r, hb, KEY0[p] + j, :],
                                     start=(j == 0), stop=(j == nk - 1))
                last.then_inc(S["pv_done"], 1)

            def na_pair(i, last):
                for u in range(16):
                    tr(i, u)
                    if u < 14:
                        qk(i, u + 2)
                    elif not last:
                        qk(i + 1, u - 14)
                    pv(i, u)

            qk(0, 0)
            qk(0, 1)
            with pe.Fori(0, NAH // 2 - 1) as i:
                na_pair(i, False)
            na_pair(NAH // 2 - 1, True)

            pe.sem_inc(S["kv_done"], 2)
            pe.sem_inc(S["num_done"], 2)
            pe.wait_ge(S["scored"], 64 + 2)
            pe.wait_ge(S["na_out_done"], 64 + 2)
            pe.wait_ge(S["pt_evicted"], 64 + 1)
            pe.wait_ge(S["ones_done"], 2)
            with pe.Fori(0, MLH // 2) as i:
                for hb in range(2):
                    h = 2 * i + hb
                    pe.wait_ge(mlsem[hb], 80 * i + 80)
                    pe.wait_ge(S["st_out"], 2 * h + 1)
                    for n in range(TT):
                        last = pe.transpose(ps[:, n // 4, (n % 4) * P:(n % 4 + 1) * P], mk[:, hb, n * P:(n + 1) * P], ident[:, :])
                    last.then_inc(S["kn_ready"], 1)
                    pe.wait_ge(S["kn_out"], 2 * h + 2)
                    for n in range(TT):
                        last = pe.matmul(ps[:, n // 4, (n % 4) * P:(n % 4 + 1) * P], mk[:, hb, n * P:(n + 1) * P],
                                         mq[:, hb, n * P:(n + 1) * P], start=True, stop=True)
                    last.then_inc(S["st_ready"], 1)
                    pe.wait_ge(S["c_zeroed"], h + 1)
                    for u in range(16):
                        n, d = ml_unit(u)
                        pe.wait_ge(S["c_updated"], 16 * h + (u + 1))
                        pe.wait_ge(S["t_done"], 16 * h + (u + 1))
                        pe.matmul(ps[:, 6 + u % 2, 0:DV + 1], mq[:, hb, n * P:(n + 1) * P], cst[:, d, :],
                                  start=True, stop=True).then_inc(S["intr_done"], 1)
                        pe.wait_ge(S["kw_done"], 16 * h + (u + 2))
                        pe.matmul(ps[:, 2 + u % 2, 0:DV + 1], kw[:, u % 2, :], mv[:, hb, n, :],
                                  start=True, stop=True).then_inc(S["kv_done"], 1)
                        pe.wait_ge(S["qkw_done"], 16 * h + (u + 3))
                        pe.wait_ge(S["hs_done"], 16 * h + (u + 1))
                        pe.matmul(ps[:, 4 + u % 2, 0:DV + 1], qkw[:, u % 2, :], mv[:, hb, n, :],
                                  start=True, stop=True).then_inc(S["num_done"], 1)

            pe.wait_ge(S["st_out"], 2 * MLH + 1)
            pe.wait_ge(S["hs_done"], 64 + 2)
            with pe.Fori(0, TT // 2) as i:
                for p in range(2):
                    T = 2 * i + p
                    pe.wait_ge(S["asm_scaled"], T + 1)
                    for g in range(4):
                        pe.wait_ge(S["mixT_lo"], 16 * T + (4 * g + 4))
                        src = mixA[p] if g < 2 else mixB[p]
                        for j in range(4):
                            at = (4 * (g % 2) + j) * P
                            last = pe.transpose(ps[:, g, j * P:(j + 1) * P], src[:, at:at + P], ident[:, :])
                        last.then_inc(S["asm_tr"], 1)

            pe.wait_ge(S["mixT_lo"], KD + KD * TT)
            with pe.Fori(BLK, BLK + OBLK) as b:
                rows_block(b, a_hi, a_lo)

            pe.wait_ge(S["bank_staged"], 8 * (BLK + OBLK))
            pe.wait_ge(S["rc_in"], 32)
            pe.sem_inc(S["r_tr"], 8)
            pe.sem_inc(S["r_logit"], 1)
            with pe.Fori(0, TT // 2) as i:
                for p in range(2):
                    T = 2 * i + p
                    pe.wait_ge(S["r_norm"], T + 1)
                    pe.wait_ge(S["r_logit"], T + 1)
                    for g in range(4):
                        for j in range(4):
                            k = 4 * g + j
                            last = pe.transpose(ps[:, g, j * P:(j + 1) * P], rh[:, p, k * P:(k + 1) * P], ident[:, :])
                        last.then_inc(S["r_tr"], 1)
                    pe.wait_ge(S["r_tA"], 2 * T + 2)
                    pe.wait_ge(S["r_tD"], 2 * T + 2)
                    for k in range(KD):
                        last = pe.matmul(ps[:, 4, bass.ds(T * NE, NE)], rT[:, k, :], wr[:, k, :], start=(k == 0), stop=(k == KD - 1),
                                         skip_group_check=True)
                    last.then_inc(S["r_logit"], 1)
            pe.wait_ge(S["affn"], 1)
            for n in range(TT):
                last = pe.transpose(ps[0:NE, n // 4, (n % 4) * P:(n % 4 + 1) * P], affs[:, n, :], ident[:, :])
                if n % 4 == 3:
                    last.then_inc(S["aff_tr"], 1)
            pe.wait_ge(S["aff_out"], 2)
            pe.wait_ge(S["affn"], 2)
            pe.transpose(ps[:, 0, 0:NE], best[:, :], ident[0:NE, 0:NE])
            pe.transpose(ps[:, 0, NE:2 * NE], bestf[:, :], ident[0:NE, 0:NE]).then_inc(S["aff_tr"], 1)

            def xt(e, g):
                if g >= 2:
                    pe.wait_ge(S["x_lo"], 4 * e + (g - 1))
                for j in range(4):
                    k = 4 * g + j
                    last = pe.transpose(ps[:, 6 + g % 2, j * P:(j + 1) * P], xg[:, k * P:(k + 1) * P], ident[:, :])
                last.then_inc(S["xtr"], 1)

            def ht(e, g):
                pe.wait_ge(S["hmul"], 2 * e + (g + 1))
                for j in range(4):
                    k = 4 * g + j
                    last = pe.transpose(ps[:, 4 + g, j * P:(j + 1) * P], hact[:, k * P:(k + 1) * P], ident[:, :])
                last.then_inc(S["htr"], 1)

            def expert(e, last_one):
                pe.wait_ge(S["x_lo"], 4 * e + 4)
                for k in range(KD):
                    pe.wait_ge(S["e_lo"], EPC * e + (2 * k + 2))
                    for a, parts in ((xh, (ehi, elo)), (xl, (ehi,))):
                        for j in range(2):
                            for c in range(2):
                                for w in parts:
                                    last = pe.matmul(ps[:, 2 * j + c, :], a[:, k, :], w[:, (2 * k + j) % ESPL, c * BW:(c + 1) * BW],
                                                     start=(k == 0 and a is xh and w is ehi), stop=(k == KD - 1 and a is xl))
                    if k < KD - 1:
                        last.then_inc(S["e_used"], 2)
                    else:
                        last.then_inc(S["gu_ready"], 1)
                pe.wait_ge(S["y_out"], 4 * e + 4)
                if not last_one:
                    pe.wait_ge(S["gathered"], 16 * e + 32)
                    xt(e + 1, 0)
                    xt(e + 1, 1)
                ht(e, 0)
                ht(e, 1)
                if not last_one:
                    xt(e + 1, 2)
                    xt(e + 1, 3)
                for k in range(KE):
                    if k % 4 == 0:
                        pe.wait_ge(S["h_lo"], 2 * e + (k // 4 + 1))
                    if k == 0:
                        pe.wait_ge(S["h_lo"], 2 * e + 2)
                        if not last_one:
                            pe.wait_ge(S["x_lo"], 4 * e + 8)
                    j0 = 2 * KD + 2 * k
                    pe.wait_ge(S["e_lo"], EPC * e + (j0 + 2))
                    for c in range(4):
                        sl = (j0 + c // 2) % ESPL
                        at = slice((c % 2) * BW, (c % 2 + 1) * BW)
                        pe.matmul(ps[:, 4 + c, :], hh[:, k, :], ehi[:, sl, at], start=(k == 0), stop=False)
                        pe.matmul(ps[:, 4 + c, :], hh[:, k, :], elo[:, sl, at], start=False, stop=False)
                        last = pe.matmul(ps[:, 4 + c, :], hl[:, k, :], ehi[:, sl, at], start=False, stop=(k == KE - 1))
                        if k == KE - 1:
                            last.then_inc(S["y_ready"], 1)
                    if k < KE - 1:
                        last.then_inc(S["e_used"], 2)

            pe.wait_ge(S["best_out"], 2)
            pe.sem_inc(S["y_out"], 4)
            pe.wait_ge(S["gathered"], 16)
            for g in range(4):
                xt(0, g)
            with pe.Fori(0, NE - 1) as e:
                expert(e, False)
            expert(NE - 1, True)


SCRATCH = {
    "rstd_d": (SEQ,), "x1": (SEQ, D), "rows": (SEQ, 3 * 1024), "feats": (24, P, SEQ), "conv": (8, P, SEQ),
    "m_rows": (8, SEQ), "decays": (8, TT), "q_rows": (2, P, SEQ), "na": (SEQ, 1024), "ml": (SEQ, 1024),
    "rpb_rep": (NAH, 15, GW, 127), "h2": (SEQ, D),
}


def kernel(x, norm_mix_g, w_in, b_gates, conv_w, conv_b, na_rpb, na_norm_g, ml_norm_g,
           w_out, norm_ffn_g, w_router, w_gate, w_up, w_down, final_norm_g):
    import concourse.bacc as bacc
    from concourse.bass_utils import run_bass_kernel_spmd

    w = w_in[0]
    cols_ = [w[:, 2048:3072], w[:, 4096:6144], w[:, 3072:4096], w[:, 0:2048]]
    w_mix = np.concatenate(cols_, axis=1).reshape(CPB, 2, P, BLK, BW).transpose(3, 0, 2, 1, 4)
    w_o = w_out[0].reshape(CPB, 2, P, OBLK, BW).transpose(3, 0, 2, 1, 4)
    ins = {
        "x": x[0], "xT": x[0].T,
        "w_stream": np.concatenate([w_mix, w_o], axis=0).reshape((BLK + OBLK) * CPB, P, 1024),
        "w_gates": w[:, 6144:6160].reshape(KD, P, 16).transpose(1, 0, 2),
        "g_mix": norm_mix_g[0].reshape(KD, P).T, "b_gates": b_gates[0],
        "conv_wb": np.concatenate([conv_w[0], conv_b], axis=0).reshape(CONVW + 1, 8, P).transpose(1, 2, 0),
        "rpb": na_rpb[0], "na_g": na_norm_g[0].reshape(8, P).T, "ml_g": ml_norm_g[0].reshape(8, P).T,
        "g_ffn": norm_ffn_g[0], "w_router": w_router[0].reshape(KD, P, NE).transpose(1, 0, 2),
        "w_gate": w_gate[0], "w_up": w_up[0], "w_down": w_down[0], "g_final": final_norm_g,
    }
    nc = bacc.Bacc("TRN2", target_bir_lowering=False, num_devices=1)
    arrays, t = {}, {}
    for name, a in ins.items():
        arrays["in_" + name] = a = np.ascontiguousarray(a)
        t[name] = nc.dram_tensor("in_" + name, a.shape, F32, kind="ExternalInput").ap()
    for name, shape in SCRATCH.items():
        t[name] = nc.dram_tensor("scr_" + name, shape, F32, kind="Internal").ap()
    t["out"] = nc.dram_tensor("out", (SEQ, D), F32, kind="ExternalOutput").ap()
    trunk(nc, t)
    r = run_bass_kernel_spmd(nc, [arrays], core_ids=[0])
    return r.results[0]["out"].reshape(1, SEQ, D)
```

```python
import math
from contextlib import ExitStack

import numpy as np

import concourse.bass as bass
from concourse import mybir
from concourse.alu_op_type import AluOpType as ALU

F32 = mybir.dt.float32
F32R = mybir.dt.float32r
U32 = mybir.dt.uint32
ACT = mybir.ActivationFunctionType
AX = mybir.AxisListType

P = 128
SEQ, D = 1024, 2048
TT = SEQ // P
KD = D // P
NAH, HD = 8, 128
GW = 64
ROWS = SEQ // GW
KR, KC = 8, 16
MLH, DK, DV = 4, 128, 256
CONVW = 5
NE, CAP, DE = 16, 128, 1024
KE = DE // P
EPS = 1e-6
NEG = -1e30
BW = 512
BLK = 12
ROWBLK = 6
OBLK = 4
CPB = KD // 2
RING = 4
GWC = KD * 16 + 32
NBH = 6 * SEQ + 2 * (14 * GW + 9 * GW + 9 * GW + 5 * P) + 64
LNS = -0.5 * math.log(DK)
GATEROW = (0, 64, 32, 96)
TOPR = CAP // 8
ERAW, ESPL = 24, 6
EARLY = 15
EPC = 2 * KD + 2 * KE


class Steps:

    def __init__(self, eng, sem, past=None):
        self.eng, self.sem, self.done, self.inside, self.turn, self.per = eng, sem, 0, 0, None, 0
        self.past = past or eng.wait_ge

    def enter(self, turn, per):
        self.turn, self.per, self.inside = turn, per, 0

    def leave(self, turns):
        assert self.inside == self.per, (self.inside, self.per)
        self.done, self.turn, self.inside = self.done + turns * self.per, None, 0

    def settle(self):
        if self.turn is None:
            self.done += 1
            self.eng.wait_ge(self.sem, self.done)
        else:
            self.inside += 1
            self.past(self.sem, self.turn * self.per + (self.done + self.inside))


def trunk(nc, t):
    ctx = ExitStack()
    with ctx:
        def sb(name, shape, dt=F32, stack=None):
            return (stack or ctx).enter_context(nc.sbuf_tensor(name, shape, dt))

        def sem(name):
            return ctx.enter_context(nc.semaphore(name))

        ident = sb("ident", [P, P])
        pad = sb("pad", [NAH * 15, 2 * GW - 1])
        half = sb("half", [P, 8])
        meansq = sb("meansq", [P, 8])
        rstd = sb("rstd", [P, 8])
        msq = sb("msq", [P, 2, 5])
        rs = sb("rs", [P, 2, 5])
        cols = sb("cols", [P, TT, 4, 2, MLH])
        decbc = sb("decbc", [P, 2, MLH, TT])

        proj = ExitStack()
        raw = sb("raw", [P, RING, 1024], F32, proj)
        whi = sb("whi", [P, RING, 1024], F32R, proj)
        wlo = sb("wlo", [P, RING, 1024], F32R, proj)
        stage = sb("stage", [P, 4, BW], F32, proj)
        t0 = sb("t0", [P, 1024], F32, proj)
        t1 = sb("t1", [P, 1024], F32, proj)
        t2 = sb("t2", [P, 1028], F32, proj)
        rstd_bc = sb("rstd_bc", [P, 1024], F32, proj)
        t3 = stage[:, 0:2, :].rearrange("p a b -> p (a b)")
        wide = ExitStack()
        a_hi = sb("a_hi", [P, KD, SEQ], F32R, wide)
        a_lo = sb("a_lo", [P, KD, SEQ], F32R, wide)
        gmix = sb("gmix", [P, KD], F32, wide)
        ssum = sb("ssum", [P, KD], F32, wide)
        wg_raw = sb("wg_raw", [P, GWC], F32, wide)
        wg_hi = sb("wg_hi", [P, GWC], F32R, wide)
        wg_lo = sb("wg_lo", [P, GWC], F32R, wide)
        wide.close()
        gate = ExitStack()
        gate.enter_context(nc.sbuf_tensor("under_wide", [P, 2 * KD * SEQ + 2 * KD + 3 * GWC], F32))
        g_bias = sb("g_bias", [P, 2], F32, gate)
        b_last = sb("b_last", [64, TT], F32, gate)
        c_last = sb("c_last", [64, TT], F32, gate)
        m_next = sb("m_next", [64, TT + 2], F32, gate)
        m_prev = sb("m_prev", [64, TT], F32, gate)
        m_end = sb("m_end", [64, TT], F32, gate)
        decay = sb("decay", [64, TT], F32, gate)
        cw = sb("cw", [P, 2, CONVW + 1], F32, gate)
        gate.close()

        nbh = ExitStack()
        na_out = sb("na_out", [P, TT, NAH * HD], F32, nbh)
        naq = sb("naq", [P, 2, SEQ], F32, nbh)
        nak = sb("nak", [P, 2, SEQ], F32, nbh)
        nav = sb("nav", [P, 2, TT, HD], F32, nbh)
        bias = sb("bias", [P, 2, 14, GW], F32, nbh)
        bias9 = sb("bias9", [P, 2, 9, GW], F32, nbh)
        prob = sb("prob", [P, 2, 9 * GW], F32, nbh)
        probT = sb("probT", [P, 2, 5, P], F32, nbh)
        top = sb("top", [P, 2], F32, nbh)
        ntop = sb("ntop", [P, 2], F32, nbh)
        psumr = sb("psumr", [P, 4], F32, nbh)
        pinv = sb("pinv", [P, 2], F32, nbh)
        nbh.close()
        mls = ExitStack()
        mls.enter_context(nc.sbuf_tensor("under_na_out", [P, TT * NAH * HD], F32))
        kn = sb("kn", [P, TT, DK], F32, mls)
        st = sb("st", [P, SEQ], F32, mls)
        wexp = sb("wexp", [P, 2, P], F32, mls)
        kw = sb("kw", [P, 2, DK], F32, mls)
        qkw = sb("qkw", [P, 2, P], F32, mls)
        inter = sb("inter", [P, 2, DV + 1], F32, mls)
        hall = sb("hall", [P, TT, 2, DV + 1], F32, mls)
        cst = sb("cst", [P, 2, DV + 1], F32, mls)
        den = sb("den", [P, TT, 2], F32, mls)
        hcols = sb("hcols", [P, 2, TT, 4, 2], F32, mls)
        hdec = sb("hdec", [P, 2, 2, TT], F32, mls)
        mls.close()
        mli = ExitStack()
        mli.enter_context(nc.sbuf_tensor("under_nbh", [P, TT * NAH * HD + NBH], F32))
        mq = sb("mq", [P, 2, SEQ], F32, mli)
        mk = sb("mk", [P, 2, SEQ], F32, mli)
        mv = sb("mv", [P, 2, TT, DV + 1], F32, mli)
        mbc = sb("mbc", [P, 2, 2, SEQ], F32, mli)
        mli.close()
        proj.close()
        gains = ExitStack()
        gains.enter_context(nc.sbuf_tensor("under_whi_end", [P, (2 * RING - 1) * 1024], F32))
        gain_na = sb("gain_na", [P, NAH * HD], F32, gains)
        gains.enter_context(nc.sbuf_tensor("under_wlo_end", [P, (RING - 1) * 1024], F32))
        gain_ml = sb("gain_ml", [P, MLH * DV], F32, gains)
        gains.close()
        gq = ExitStack()
        gq.enter_context(nc.sbuf_tensor("under_t0", [P, 3 * RING * 1024 + 4 * BW], F32))
        qrows = sb("qrows", [P, 2, SEQ], F32, gq)
        gq.close()
        mlo = ExitStack()
        mlo.enter_context(nc.sbuf_tensor("under_stage", [P, 3 * RING * 1024 + 4 * BW], F32))
        mh = sb("mh", [P, 2, TT, DV], F32, mlo)
        mlo.close()

        exps = ExitStack()
        gbc = sb("gbc", [P, D], F32, exps)
        wr = sb("wr", [P, KD, NE], F32, exps)
        rsmall = sb("rsmall", [P, 8], F32, exps)
        gateT = sb("gateT", [P, NE], F32, exps)
        tokT = sb("tokT", [P, NE], U32, exps)
        tokg = sb("tokg", [P, 1], U32, exps)
        toks = sb("toks", [P, 1], U32, exps)
        gcol = sb("gcol", [P, 1], F32, exps)
        smx = sb("smx", [P, TT], F32, exps)
        affs = sb("affs", [P, TT, NE], F32, exps)
        ehi = sb("ehi", [P, ESPL, 1024], F32R, exps)
        elo = sb("elo", [P, ESPL, 1024], F32R, exps)
        under = ExitStack()
        eraw = sb("eraw", [P, ERAW, 1024], F32, under)
        xg = sb("xg", [P, D], F32, under)
        xh = sb("xh", [P, KD, P], F32R, under)
        xl = sb("xl", [P, KD, P], F32R, under)
        hact = sb("hact", [P, DE], F32, under)
        hh = sb("hh", [P, KE, P], F32R, under)
        hl = sb("hl", [P, KE, P], F32R, under)
        ey = sb("ey", [P, D], F32, under)
        under.close()
        over = ExitStack()
        over.enter_context(nc.sbuf_tensor("under_early", [P, EARLY * 1024], F32))
        rx = sb("rx", [P, 4, D], F32, over)
        squares = sb("squares", [P, D], F32, over)
        rh = sb("rh", [P, 2, D], F32, over)
        rT = sb("rT", [P, 2, KD, P], F32, over)
        affT = sb("affT", [NE, SEQ], F32, over)
        best = sb("best", [NE, CAP], F32, over)
        besti = sb("besti", [NE, CAP], U32, over)
        bestf = sb("bestf", [NE, CAP], F32, over)
        over.close()
        exps.close()

        ps = ctx.enter_context(nc.psum_tensor("ps", [P, 8, BW], F32))

        S = {}
        for n in ("const_in ident_done raw0 raw1 raw2 raw3 xt0 xt1 xnat0 xnat1 xn_sq hT_hi hT_lo w_hi w_lo w_used "
                  "bank_ready bank_staged st0 st1 st2 st3 stage_free meansq_done rstd_done rstd_out rstd_bc_in "
                  "wg_hi wg_done gates_ready gates_copied gpad_zero gb_in grows_out dve_step "
                  "act_step pool_step mask_done acc_free conv_in conv_free silu_done conv_out feats_out x1_init "
                  "pool_past dve_past pad_in rep_out cols_ready cols_out nq0 nq1 nkv0 nkv1 nb0 nb1 q_scaled "
                  "bias_ready qk_done scored na_max exp_done transposed pt_evicted pv_done na_step na_out_done "
                  "na_saved ml0 ml1 hcols_ready kn_ready den_done fwd_out kn_out st_ready st_out wexp_done masked kw_done qkw_done "
                  "kv_done num_done xa0 xa1 rs_done asm_stats gain_in asm_gate asm_mean asm_scaled asm_tr mixT_hi mixT_lo "
                  "rc_in rx0 rx1 rx2 rx3 r_sq r_mean r_rstd r_norm rh_free r_tr r_tA r_tD r_logit smax r_exp affn aff_tr "
                  "aff_out best_out e_hi e_lo e_used gu_ready silu2 hmul xtr x_hi x_lo htr h_hi "
                  "h_lo y_ready y_out tokg_done toks_done gcol_done gathered scattered ey_free intr_done t_done "
                  "c_zeroed c_updated hs_done ml_head_done ml_saved mh_free ones_done gate_act gate_arg gate_out "
                  "gates_in h_out0 h_out1").split():
            S[n] = sem(n)
        rawsem = [S[f"raw{i}"] for i in range(4)]
        stsem = [S[f"st{i}"] for i in range(4)]
        xtsem = [S["xt0"], S["xt1"]]
        xnatsem = [S["xnat0"], S["xnat1"]]
        xhalf = [t2[:, 0:1024], rstd_bc[:, :]]
        houtsem = [S["h_out0"], S["h_out1"]]
        xasem = [S["xa0"], S["xa1"]]
        rxsem = [S[f"rx{i}"] for i in range(4)]
        nqsem, nkvsem, nbsem, mlsem = ([S[n + "0"], S[n + "1"]] for n in ("nq", "nkv", "nb", "ml"))
        ersem = rawsem + nqsem + nkvsem + nbsem + mlsem
        ER0 = [32 * (BLK + OBLK)] * RING + [16 * (NAH // 2)] * 2 + [32 * (NAH // 2)] * 4 + [80 * (MLH // 2)] * 2
        KEY0 = [0, 0, 0, 1, 2, 3, 4, 4]
        BROW = [7, 5, 3, 3, 3, 3, 3, 1]
        WIDE = [8 * GW, 8 * GW] + [9 * GW] * 4 + [8 * GW, 8 * GW]

        def flat2(a):
            return a.rearrange("p a b -> p (a b)")

        def by_chunk(bank):
            return bank.rearrange("p (k c) -> p k c", c=P)

        SC = [flat2(ps[:, 0:2, :]), flat2(ps[:, 2:4, :])]
        PTP = flat2(ps[:, 4:6, :])

        mixA = [t0[:, :], flat2(stage[:, 0:2, :])]
        mixB = [t2[:, 0:1024], rstd_bc[:, :]]
        mixO = [t1[:, :], flat2(stage[:, 2:4, :])]

        def used(e, j):
            if j in (30, 31):
                return S["gu_ready"], e + 1
            if j in (46, 47):
                return S["y_ready"], 4 * e + 4
            return S["e_used"], 44 * e + (j + 1 if j < 30 else j - 1)

        def ml_unit(u):
            return (u // 2, 0) if u % 2 == 0 else (TT - 1 - u // 2, 1)

        def chunk_free(eng, b, m):
            if m >= 4:
                eng.wait_ge(S["w_used"], 7 * b + (m - 3))
            elif m < 3:
                eng.wait_ge(S["w_used"], 7 * b + (m - 2))
            else:
                eng.wait_ge(S["bank_ready"], 8 * b)

        TRBANK = (0, 1, 2, 3, 6, 7)

        block = ctx.enter_context(nc.Block())

        @block.sync
        def _(sp):
            def fetch(b, m):
                if not (isinstance(b, int) and b == 0 and m < 4):
                    sp.wait_ge(S["w_lo"], CPB * b + (m - 3))
                src = t["w_stream"][bass.ds(CPB * b + m, 1), :, :].rearrange("a p c -> (a p) c")
                sp.dma_start(raw[:, m % RING, :], src).then_inc(rawsem[m % RING], 16)

            sp.dma_start(gmix[:, :], t["g_mix"]).then_inc(S["const_in"], 16)
            sp.dma_start(wg_raw[:, 0:KD * 16], t["w_gates"]).then_inc(S["const_in"], 16)
            for m in range(CPB):
                fetch(0, m)
                for k in (2 * m, 2 * m + 1):
                    if k >= 2:
                        sp.wait_ge(S["hT_lo"], k - 1)
                    sp.dma_start((t0, t1)[k % 2][:, :], t["xT"][k * P:(k + 1) * P, :]).then_inc(xtsem[k % 2], 16)
            with sp.Fori(1, BLK) as b:
                for m in range(CPB):
                    fetch(b, m)
            for m in range(RING):
                fetch(BLK, m)

            sp.wait_ge(S["bank_ready"], 8 * BLK)
            sp.wait_ge(S["rep_out"], 16)

            def fetch_bias(i, hb):
                h = 2 * i + hb
                for r in range(2):
                    at = bass.AP(t["rpb_rep"].tensor, h * (15 * GW * 127) + ((1 - r) * GW * 127 + GW - 1),
                                 [[126, GW], [GW * 127, 14], [1, GW]])
                    sp.dma_start(bias[r * GW:(r + 1) * GW, hb, :, :], at).then_inc(nbsem[hb], 16)

            def fetch_head(i, hb):
                feats = t["feats"]
                q = feats[bass.ds(2 * i + (hb + 8), 1), :, :].rearrange("a p c -> (a p) c")
                k = feats[bass.ds(2 * i + (hb + 16), 1), :, :].rearrange("a p c -> (a p) c")
                v = t["rows"].rearrange("(n p) c -> p n c", p=P)[:, :, bass.ds((2 * i + hb) * HD, HD)]
                sp.dma_start(naq[:, hb, :], q).then_inc(nqsem[hb], 16)
                sp.dma_start(nak[:, hb, :], k).then_inc(nkvsem[hb], 16)
                sp.dma_start(nav[:, hb, :, :], v).then_inc(nkvsem[hb], 16)

            def fetch_ml(h):
                hb = h % 2
                sp.dma_start(mq[:, hb, :], t["conv"][h, :, :]).then_inc(mlsem[hb], 16)
                sp.dma_start(mk[:, hb, :], t["conv"][MLH + h, :, :]).then_inc(mlsem[hb], 16)
                sp.dma_start(mv[:, hb, :, 0:DV], t["rows"].rearrange("(n p) c -> p n c", p=P)
                             [:, :, 1024 + h * DV:1024 + (h + 1) * DV]).then_inc(mlsem[hb], 16)
                for d in range(2):
                    sp.dma_start(mbc[:, hb, d, :], t["m_rows"][d * MLH + h, :].partition_broadcast(P)).then_inc(mlsem[hb], 16)

            sp.wait_ge(S["bank_staged"], 8 * BLK - 1)
            for m in stsem:
                sp.wait_ge(m, 32 * (BLK - 1))
            sp.wait_ge(S["conv_out"], 16 * 8)
            fetch_head(0, 0)
            fetch_bias(0, 0)
            sp.dma_start(qrows[:, :, :], t["q_rows"].rearrange("a p c -> p a c")).then_inc(S["gates_in"], 16)
            sp.dma_start(decbc[:, :, :, :].rearrange("p d h n -> p (d h n)"),
                         t["decays"].rearrange("a n -> (a n)").partition_broadcast(P)).then_inc(S["gates_in"], 16)
            fetch_head(0, 1)
            fetch_bias(0, 1)
            sp.wait_ge(S["feats_out"], 1)
            sp.dma_start(gain_na[:, :], t["na_g"].partition_broadcast(P)).then_inc(S["gain_in"], 16)
            sp.dma_start(gain_ml[:, :], t["ml_g"].partition_broadcast(P)).then_inc(S["gain_in"], 16)
            fetch_ml(0)
            fetch_ml(1)
            with sp.Fori(1, NAH // 2) as i:
                for hb in range(2):
                    sp.wait_ge(S["pv_done"], 16 * i + (8 * hb - 8 + 2))
                    fetch_bias(i, hb)
                    fetch_head(i, hb)
            sp.wait_ge(S["na_out_done"], 64 + 2)
            sp.dma_start(t["na"].rearrange("(n p) c -> p n c", p=P), na_out[:, :, :]).then_inc(S["na_saved"], 16)

            sp.sem_inc(S["mh_free"], 2)

            def fetch_mix(i, p, wait=True, parts="OAB"):
                rows = bass.ds((2 * i + p) * P, P)
                if "O" in parts:
                    if wait:
                        sp.wait_ge(S["asm_scaled"], 2 * i + (p - 1))
                    sp.dma_start(mixO[p], t["rows"][rows, 2048:3072]).then_inc(xasem[p], 16)
                if "A" in parts:
                    if wait:
                        sp.wait_ge(S["asm_tr"], 8 * i + (4 * p - 6))
                    sp.dma_start(mixA[p], t["na"][rows, :]).then_inc(xasem[p], 16)
                if "B" in parts:
                    if wait:
                        sp.wait_ge(S["asm_tr"], 8 * i + (4 * p - 4))
                    sp.dma_start(mixB[p], t["ml"][rows, :]).then_inc(xasem[p], 16)

            for h in range(MLH):
                if h == MLH - 1:
                    sp.wait_ge(S["na_saved"], 16)
                    for p in range(2):
                        fetch_mix(0, p, wait=False, parts="OA")
                sp.wait_ge(S["ml_head_done"], h + 1)
                sp.dma_start(t["ml"].rearrange("(n p) c -> p n c", p=P)[:, :, h * DV:(h + 1) * DV], mh[:, h % 2, :, :])\
                    .then_inc(S["ml_saved"], 16)
                sp.wait_ge(S["ml_saved"], 16 * (h + 1))
                sp.sem_inc(S["mh_free"], 1)
                if h + 2 < MLH:
                    fetch_ml(h + 2)

            for p in range(2):
                fetch_mix(0, p, wait=False, parts="B")
            with sp.Fori(1, TT // 2) as i:
                for p in range(2):
                    fetch_mix(i, p)
            for m in range(RING, CPB):
                fetch(BLK, m)
            with sp.Fori(BLK + 1, BLK + OBLK) as b:
                for m in range(CPB):
                    fetch(b, m)

            sp.wait_ge(S["bank_ready"], 8 * (BLK + OBLK))
            sp.dma_start(gbc[:, :], t["g_ffn"].partition_broadcast(P)).then_inc(S["rc_in"], 16)
            sp.dma_start(wr[:, :, :], t["w_router"]).then_inc(S["rc_in"], 16)

            def fetch_x1(T):
                if T < TT:
                    sp.wait_ge(stsem[T % 4], 32 * (BLK + OBLK - 1) + 16 * (T // 4 + 1))
                sp.dma_start(rx[:, T % 4, :], t["x1"][(T % TT) * P:(T % TT + 1) * P, :]).then_inc(rxsem[T % 4], 16)

            def store_normed(T, dst):
                sp.wait_ge(S["r_norm"], T + 1)
                sp.dma_start(t[dst][(T % TT) * P:(T % TT + 1) * P, :], rh[:, T % 2, :]).then_inc(houtsem[T % 2], 16)

            def normed_free(T):
                sp.wait_ge(houtsem[T % 2], 16 * (T // 2 + 1))
                sp.sem_inc(S["rh_free"], 1)

            def fetch_piece(e, j):
                if not (isinstance(e, int) and e == 0 and j < ERAW):
                    sp.wait_ge(S["e_lo"], EPC * e + (j - ERAW + 1))
                k = j // 2 if j < 2 * KD else (j - 2 * KD) // 2
                if j < 2 * KD:
                    src = t[("w_gate", "w_up")[j % 2]][bass.ds(e, 1), k * P:(k + 1) * P, :]
                else:
                    src = t["w_down"][bass.ds(e, 1), k * P:(k + 1) * P, (j % 2) * 1024:(j % 2 + 1) * 1024]
                sp.dma_start(eraw[:, j % ERAW, :], src.rearrange("a p c -> (a p) c")).then_inc(ersem[(j // 2) % (ERAW // 2)], 16)

            sp.sem_inc(S["rh_free"], 2)
            for T in range(4):
                fetch_x1(T)
            early = 0
            for T in range(TT):
                store_normed(T, "h2")
                if T + 4 < TT:
                    fetch_x1(T + 4)
                if T >= 4:
                    for j in range(early, min(early + 4, EARLY)):
                        fetch_piece(0, j)
                    early = min(early + 4, EARLY)
                if T:
                    normed_free(T - 1)
            normed_free(TT - 1)
            sp.wait_ge(S["r_logit"], TT + 1)
            for j in range(EARLY, ERAW):
                fetch_piece(0, j)
            sp.dma_start(gbc[:, :], t["g_final"].partition_broadcast(P)).then_inc(S["rc_in"], 16)

            for j in range(ERAW, EPC):
                fetch_piece(0, j)
            with sp.Fori(1, NE) as e:
                for j in range(EPC):
                    fetch_piece(e, j)

            sp.wait_ge(S["ey_free"], NE + 1)
            for T in range(TT, TT + 4):
                fetch_x1(T)
            for T in range(TT, 2 * TT):
                store_normed(T, "out")
                if T + 4 < 2 * TT:
                    fetch_x1(T + 4)
                if T > TT:
                    normed_free(T - 1)
            normed_free(2 * TT - 2)
            normed_free(2 * TT - 1)

        @block.gpsimd
        def _(pool):
            def past(s, v):
                pool.wait_ge(s, v)
                pool.sem_inc(S["pool_past"], 1)

            step = Steps(pool, S["pool_step"], past)

            pool.memset(ident[:, :], 0.0).then_inc(S["pool_step"], 1)
            step.settle()
            pool.affine_select(out=ident[:, :], in_=ident[:, :], compare_op=ALU.not_equal, fill=1.0, base=0,
                               pattern=[[-1, P]], channel_multiplier=1).then_inc(S["ident_done"], 1)
            pool.memset(half[:, :], -0.5).then_inc(S["pool_step"], 1)
            step.settle()
            pool.memset(pad[:, :], NEG).then_inc(S["pool_step"], 1)
            step.settle()
            pool.memset(wg_raw[:, KD * 16:GWC], 0.0).then_inc(S["gpad_zero"], 1)
            pool.dma_start(pad[:, GW - KC:GW + KC - 1], t["rpb"].rearrange("h r c -> (h r) c")).then_inc(S["pad_in"], 16)
            for k in range(KD):
                if k >= 2:
                    pool.wait_ge(S["xn_sq"], k - 1)
                pool.dma_start(xhalf[k % 2], t["x"][(k // 2) * P:(k // 2 + 1) * P,
                                                    (k % 2) * 1024:(k % 2 + 1) * 1024]).then_inc(xnatsem[k % 2], 16)
            pool.wait_ge(S["meansq_done"], 1)
            pool.tensor_tensor(rstd[:, :], meansq[:, :], half[:, :], ALU.pow).then_inc(S["rstd_done"], 1)
            pool.wait_ge(S["rstd_done"], 1)
            pool.dma_start(t["rstd_d"].rearrange("(t p) -> p t", p=P), rstd[:, :],
                           allow_slow_non_contiguous=True).then_inc(S["rstd_out"], 16)
            pool.wait_ge(S["rstd_out"], 16)
            pool.dma_start(rstd_bc[:, :], t["rstd_d"].partition_broadcast(P)).then_inc(S["rstd_bc_in"], 16)
            pool.memset(g_bias[:, :], 0.0).then_inc(S["pool_step"], 1)
            step.settle()
            for q, at in enumerate(GATEROW):
                pool.memset(g_bias[at:at + MLH, 0:1], 1.0).then_inc(S["gpad_zero"], 1)
                pool.dma_start(g_bias[at:at + MLH, 1:2], t["b_gates"][4 * q:4 * q + 4].unsqueeze(1)).then_inc(S["gb_in"], 16)
            pool.wait_ge(S["gpad_zero"], 5)
            for s in (b_last, c_last, m_prev):
                pool.memset(s[:, :], 0.0).then_inc(S["gpad_zero"], 1)
            pool.memset(m_next[:, :], 0.0).then_inc(S["gpad_zero"], 1)

            def store(b, dst, accum=False):
                for n in range(8):
                    past(S["bank_staged"], 8 * b + (n + 1))
                    if accum:
                        pool.dma_start(dst(b, n), stage[:, n % 4, :], accum_op=ALU.add).then_inc(stsem[n % 4], 16)
                    else:
                        pool.dma_start(dst(b, n), stage[:, n % 4, :]).then_inc(stsem[n % 4], 16)
                    for o in (n - 2,) if n < 7 else (5, 6, 7):
                        if o >= 0:
                            past(stsem[o % 4], 32 * b + 16 * (o // 4 + 1))
                            pool.sem_inc(S["stage_free"], 1)

            def to_rows(b, n):
                return t["rows"][n * P:(n + 1) * P, bass.ds(b * BW, BW)]

            def to_feats(b, n):
                g, hh_ = n // 2, n % 2
                return t["feats"][bass.ds(4 * b + (g - 4 * ROWBLK), 1), :, hh_ * BW:(hh_ + 1) * BW]\
                    .rearrange("a p c -> (a p) c")

            with pool.Fori(0, ROWBLK) as b:
                store(b, to_rows)

            pool.memset(t3, 1.0).then_inc(S["pool_step"], 1)
            step.settle()
            pool.memset(t3.rearrange("p (n j) -> p n j", j=P)[:, :, 0:1], 0.0).then_inc(S["mask_done"], 1)
            pool.wait_ge(S["gate_act"], 5)
            for d in range(2):
                pool.dma_start(t["m_rows"][d * MLH:(d + 1) * MLH, :], t2[32 * d:32 * d + MLH, 0:1024]).then_inc(S["gate_out"], 16)
                pool.dma_start(t["decays"][d * MLH:(d + 1) * MLH, :], decay[32 * d:32 * d + MLH, :]).then_inc(S["gate_out"], 16)
            pool.dma_start(t["q_rows"][0, :, :], t0[:, :]).then_inc(S["gate_out"], 16)
            pool.dma_start(t["q_rows"][1, :, :], t1[:, :]).then_inc(S["gate_out"], 16)
            pool.wait_ge(S["gate_out"], 96)
            pool.sem_inc(S["acc_free"], 1)
            pool.wait_ge(S["pad_in"], 16)
            pool.dma_start(t["rpb_rep"].rearrange("h r c j -> (h r) c j"),
                           pad[:, :].unsqueeze(1).broadcast_to([NAH * 15, GW, 2 * GW - 1])).then_inc(S["rep_out"], 16)

            with pool.Fori(ROWBLK, ROWBLK + 2) as b:
                store(b, to_feats)
            with pool.Fori(ROWBLK + 2, BLK) as b:
                for q in range(2):
                    c = 2 * b + (q - 2 * (ROWBLK + 2))
                    past(S["conv_free"], c + 1)
                    pool.dma_start(t2[:, 2:1026], t["feats"][bass.ds(c, 1), :, :].rearrange("a p c -> (a p) c"))\
                        .then_inc(S["conv_in"], 16)
                    pool.dma_start(cw[:, q, :], t["conv_wb"][bass.ds(c, 1), :, :].rearrange("a p c -> (a p) c"))\
                        .then_inc(S["conv_in"], 16)
                    tile = bass.ds(P * c, P)
                    pool.dma_start(t["x1"][tile, :], t["x"][tile, :]).then_inc(S["x1_init"], 16)
                    past(S["silu_done"], c + 1)
                    pool.dma_start(t["conv"][bass.ds(c, 1), :, :].rearrange("a p c -> (a p) c"), t0[:, :])\
                        .then_inc(S["conv_out"], 16)
                    past(S["conv_out"], 16 * c + 16)
                    pool.sem_inc(S["acc_free"], 1)
                store(b, to_feats)
            pool.sem_inc(S["feats_out"], 1)

            def prepare(i, hb, first):
                if first:
                    pool.wait_ge(nqsem[hb], 16)
                else:
                    past(nqsem[hb], 16 * i + 16)
                pool.tensor_scalar(naq[:, hb, :], naq[:, hb, :], HD ** -0.5, 0.0, ALU.mult, ALU.add).then_inc(S["q_scaled"], 1)
                if first:
                    pool.wait_ge(nbsem[hb], 32)
                else:
                    past(nbsem[hb], 32 * i + 32)
                for r in range(2):
                    rows = slice(r * GW, (r + 1) * GW)
                    a, b = bias[rows, hb, :, 0:GW - KC], bias[rows, hb, :, KC:GW]
                    pool.affine_select(out=a, in_=a, compare_op=ALU.is_ge, fill=NEG, base=KC // 2,
                                       pattern=[[0, 14], [1, GW - KC]], channel_multiplier=-1).then_inc(S["pool_step"], 1)
                    step.settle()
                    pool.affine_select(out=b, in_=b, compare_op=ALU.is_ge, fill=NEG, base=KC // 2 - 1 - KC,
                                       pattern=[[0, 14], [-1, GW - KC]], channel_multiplier=1).then_inc(S["pool_step"], 1)
                    step.settle()
                pool.tensor_copy(bias9[:, hb, :, :], bias[:, hb, 2:11, :]).then_inc(S["pool_step"], 1)
                step.settle()
                for r, a in enumerate((8, 0)):
                    pool.memset(bias9[r * GW:(r + 1) * GW, hb, a, :], NEG).then_inc(S["bias_ready"], 1)
                    if first:
                        pool.wait_ge(S["bias_ready"], 2 * hb + r + 1)
                    else:
                        past(S["bias_ready"], 4 * i + (2 * hb + r + 1))

            pool.wait_ge(S["bank_ready"], 8 * BLK)
            for hb in range(2):
                pool.memset(mv[:, hb, :, DV:DV + 1], 1.0).then_inc(S["ones_done"], 1)
            for hb in range(2):
                prepare(0, hb, True)
            with pool.Fori(1, NAH // 2) as i:
                step.enter(i - 1, 10)
                prepare(i, 0, False)
                prepare(i, 1, False)
                step.leave(NAH // 2 - 1)

            pool.wait_ge(S["na_out_done"], 64 + 2)
            pool.sem_inc(S["kw_done"], 1)
            with pool.Fori(0, MLH // 2) as i:
                for hb in range(2):
                    h = 2 * i + hb
                    past(S["kn_out"], 2 * h + 2)
                    past(S["hcols_ready"], 2 * h + 2)
                    for u in range(16):
                        n, d = ml_unit(u)
                        past(S["kv_done"], 16 * h + (u + 1))
                        pool.tensor_scalar(kw[:, u % 2, :], kn[:, n, :], hcols[:, hb, n, 1, d:d + 1], 0.0, ALU.mult, ALU.add)\
                            .then_inc(S["kw_done"], 1)
                        past(S["wexp_done"], 16 * h + (u + 1))
                        a = wexp[:, u % 2, :]
                        way = 1 if d == 0 else -1
                        pool.affine_select(out=a, in_=a, compare_op=ALU.is_ge, fill=0.0, base=0,
                                           pattern=[[way, P]], channel_multiplier=-way).then_inc(S["masked"], 1)

            pool.wait_ge(S["gain_in"], 32)
            with pool.Fori(0, TT // 2) as i:
                for p in range(2):
                    past(xasem[p], 48 * i + 48)
                    pool.tensor_tensor(mixO[p], mixO[p], gain_ml[:, :], ALU.mult).then_inc(S["asm_gate"], 1)
                    pool.wait_ge(S["asm_mean"], 2 * i + (p + 1))
                    pool.tensor_tensor(rs[:, p, :], msq[:, p, :], half[:, 0:5], ALU.pow).then_inc(S["rs_done"], 1)

            pool.wait_ge(S["x1_init"], 16 * TT)

            def to_x1(b, n):
                return t["x1"][n * P:(n + 1) * P, bass.ds((b - BLK) * BW, BW)]

            with pool.Fori(BLK, BLK + OBLK) as b:
                store(b, to_x1, accum=True)

            with pool.Fori(0, TT // 4) as i:
                for p in range(4):
                    pool.wait_ge(S["r_mean"], 4 * i + (p + 1))
                    pool.tensor_tensor(rstd[:, p:p + 1], rsmall[:, 4 + p:5 + p], half[:, 0:1], ALU.pow).then_inc(S["r_rstd"], 1)

            pool.sem_inc(S["ey_free"], 1)
            pool.wait_ge(S["best_out"], 2)
            pool.wait_ge(S["rh_free"], 2 + TT)

            def gather(e):
                pool.tensor_copy(tokg[:, :], tokT[:, bass.ds(e, 1)]).then_inc(S["tokg_done"], 1)
                if isinstance(e, int):
                    pool.wait_ge(S["tokg_done"], e + 1)
                else:
                    past(S["tokg_done"], e + 1)
                pool.indirect_dma_start(out=xg[:, :], out_offset=None, in_=t["h2"],
                                        in_offset=bass.IndirectOffsetOnAxis(ap=tokg[:, 0:1], axis=0)).then_inc(S["gathered"], 16)

            def add_outputs(e):
                past(S["y_out"], 4 * e + 8)
                pool.indirect_dma_start(out=t["x1"], out_offset=bass.IndirectOffsetOnAxis(ap=toks[:, 0:1], axis=0),
                                        in_=ey[:, :], in_offset=None, compute_op=ALU.add).then_inc(S["scattered"], 16)
                past(S["scattered"], 16 * e + 16)
                pool.sem_inc(S["ey_free"], 1)

            def columns(e):
                pool.tensor_copy(toks[:, :], tokT[:, bass.ds(e, 1)]).then_inc(S["toks_done"], 1)
                pool.tensor_copy(gcol[:, :], gateT[:, bass.ds(e, 1)]).then_inc(S["gcol_done"], 1)
                past(S["toks_done"], e + 1)

            gather(0)
            with pool.Fori(0, NE - 1) as e:
                past(S["xtr"], 4 * e + 4)
                past(S["gathered"], 16 * e + 16)
                gather(e + 1)
                columns(e)
                add_outputs(e)
            columns(NE - 1)
            add_outputs(NE - 1)

            with pool.Fori(TT // 4, TT // 2) as i:
                for p in range(4):
                    pool.wait_ge(S["r_mean"], 4 * i + (p + 1))
                    pool.tensor_tensor(rstd[:, p:p + 1], rsmall[:, 4 + p:5 + p], half[:, 0:1], ALU.pow).then_inc(S["r_rstd"], 1)

        @block.scalar
        def _(act):
            step = Steps(act, S["act_step"])

            def high(b, m):
                act.wait_ge(rawsem[m % RING], 32 * b + 16 * (m // RING + 1))
                if not (isinstance(b, int) and b == 0 and m < 4):
                    chunk_free(act, b, m)
                act.activation(whi[:, m % RING, :], raw[:, m % RING, :], ACT.Copy).then_inc(S["w_hi"], 1)

            def evict_rows(b, func=ACT.Copy):
                for n in range(8):
                    act.wait_ge(S["bank_ready"], 8 * b + (n + 1))
                    if not (isinstance(b, int) and b == 0 and n < 4):
                        act.wait_ge(S["stage_free"], 8 * b + (n - 3))
                    act.activation(stage[:, n % 4, :], ps[:, n, :], func, scale=rstd[:, n:n + 1])\
                        .then_inc(S["bank_staged"], 1)

            act.wait_ge(S["const_in"], 32)
            act.wait_ge(S["gpad_zero"], 1)
            act.activation(wg_hi[:, :], wg_raw[:, :], ACT.Copy).then_inc(S["wg_hi"], 1)
            for k in range(KD):
                if k % 2 == 0 :
                    high(0, k // 2)
                act.wait_ge(xtsem[k % 2], 16 * (k // 2 + 1))
                act.activation(a_hi[:, k, :], (t0, t1)[k % 2][:, :], ACT.Copy, scale=gmix[:, k:k + 1]).then_inc(S["hT_hi"], 1)
                act.wait_ge(xnatsem[k % 2], 16 * (k // 2 + 1))
                act.activation(xhalf[k % 2], xhalf[k % 2], ACT.Square, accum_out=ssum[:, k:k + 1]).then_inc(S["xn_sq"], 1)
            for m in range(3):
                high(1, m)
            act.wait_ge(S["rstd_done"], 1)
            evict_rows(0)
            for first, end, func in ((1, ROWBLK - 2, ACT.Copy), (ROWBLK - 2, ROWBLK, ACT.Sigmoid)):
                with act.Fori(first, end) as b:
                    for m in range(3, CPB):
                        high(b, m)
                    for m in range(3):
                        high(b + 1, m)
                    evict_rows(b, func)

            high(ROWBLK, 3)
            act.wait_ge(S["gate_arg"], 1)
            act.activation(t2[0:64, 0:1024], t2[0:64, 0:1024], ACT.Exp, scale=-1.0).then_inc(S["act_step"], 1)
            step.settle()
            act.activation(t2[0:64, 0:1024], t2[0:64, 0:1024], ACT.Ln, bias=1.0).then_inc(S["gate_act"], 1)
            high(ROWBLK, 4)
            act.wait_ge(S["gate_arg"], 2)
            act.activation(decay[:, :], decay[:, :], ACT.Exp).then_inc(S["gate_act"], 1)
            high(ROWBLK, 5)
            act.wait_ge(S["gate_arg"], 3)
            act.activation(t1[64:128, :], t3[0:64, :], ACT.Exp, scale=-1.0).then_inc(S["gate_act"], 1)
            act.wait_ge(S["gate_arg"], 4)
            act.activation(t0[64:128, :], t3[0:64, :], ACT.Exp).then_inc(S["gate_act"], 1)
            act.wait_ge(S["gate_arg"], 5)
            act.activation(t1[0:64, :], t3[0:64, :], ACT.Exp).then_inc(S["gate_act"], 1)
            for m in range(6, CPB):
                high(ROWBLK, m)
            for m in range(CPB):
                high(ROWBLK + 1, m)
            for m in range(3):
                high(ROWBLK + 2, m)
            with act.Fori(ROWBLK + 2, BLK) as b:
                for m in range(3, CPB):
                    high(b, m)
                    if m in (5, 7):
                        q = (m - 5) // 2
                        act.wait_ge(S["conv_free"], 2 * b + (q - 2 * (ROWBLK + 2) + 2))
                        act.activation(t0[:, :], t0[:, :], ACT.Silu, bias=cw[:, q, CONVW:CONVW + 1]).then_inc(S["silu_done"], 1)
                for m in range(3):
                    high(b + 1, m)

            act.sem_inc(S["pt_evicted"], 1)

            def expo(i, u):
                act.wait_ge(S["na_max"], 16 * i + (u + 1))
                w = WIDE[u % 8]
                act.activation(prob[:, u % 2, 0:w], prob[:, u % 2, 0:w], ACT.Exp, bias=ntop[:, u % 2:u % 2 + 1],
                               accum_out=psumr[:, u % 4:u % 4 + 1]).then_inc(S["exp_done"], 1)

            def evict_pt(i, u):
                act.wait_ge(S["transposed"], 16 * i + (u + 3))
                act.wait_ge(S["pv_done"], 16 * i + (u + 1))
                full = act.activation(flat2(probT[:, u % 2, 0:4, :]), PTP[:, 0:4 * P], ACT.Copy)
                if WIDE[u % 8] > 4 * P:
                    full = act.activation(probT[0:GW, u % 2, 4, :], PTP[0:GW, 4 * P:5 * P], ACT.Copy)
                full.then_inc(S["pt_evicted"], 1)

            def na_pair(i, last):
                for u in range(16):
                    evict_pt(i, u)
                    if u < 14:
                        expo(i, u + 2)
                    elif not last:
                        expo(i + 1, u - 14)

            expo(0, 0)
            expo(0, 1)
            with act.Fori(0, NAH // 2 - 1) as i:
                na_pair(i, False)
            na_pair(NAH // 2 - 1, True)

            act.sem_inc(S["t_done"], 2)
            with act.Fori(0, MLH // 2) as i:
                for hb in range(2):
                    h = 2 * i + hb
                    act.wait_ge(mlsem[hb], 80 * i + 80)
                    act.wait_ge(S["hcols_ready"], 2 * h + 2)

                    def weight(u):
                        n, d = ml_unit(u)
                        act.wait_ge(S["qkw_done"], 16 * h + (u + 1))
                        act.activation(wexp[:, u % 2, :], mbc[:, hb, d, n * P:(n + 1) * P], ACT.Exp, scale=-1.0,
                                       bias=hcols[:, hb, n, 0, d:d + 1]).then_inc(S["wexp_done"], 1)

                    weight(0)
                    act.wait_ge(S["st_ready"], h + 1)
                    for j in range(2):
                        act.wait_ge(S["qkw_done"], 16 * h + 2)
                        act.activation(st[:, j * BW:(j + 1) * BW], ps[:, 4 + j, :], ACT.Copy).then_inc(S["st_out"], 1)
                    for u in range(16):
                        n, d = ml_unit(u)
                        if u < 15:
                            weight(u + 1)
                        act.wait_ge(S["intr_done"], 16 * h + (u + 1))
                        act.wait_ge(S["hs_done"], 16 * h + (u + 1))
                        act.activation(inter[:, u % 2, :], ps[:, 6 + u % 2, 0:DV + 1], ACT.Copy,
                                       scale=hcols[:, hb, n, 2, d:d + 1]).then_inc(S["t_done"], 1)
                    act.wait_ge(S["den_done"], h + 1)
                    act.wait_ge(S["mh_free"], h + 1)
                    for n in range(TT):
                        act.activation(mh[:, hb, n, :], hall[:, n, 0, 0:DV], ACT.Copy, scale=den[:, n, 0:1]).then_inc(S["fwd_out"], 1)

            act.wait_ge(S["mh_free"], 2 + MLH)
            act.wait_ge(S["na_saved"], 16)
            act.wait_ge(S["hs_done"], 64 + 2)

            def stats(i, p):
                act.wait_ge(xasem[p], 48 * i + 48)
                if not (isinstance(i, int) and i == 0 and p == 0):
                    act.wait_ge(S["asm_stats"], 2 * i + p)
                act.activation(flat2(ps[:, 4:6, :]), mixA[p], ACT.Square, accum_out=msq[:, p, 0:1])
                for h in range(MLH):
                    last = act.activation(ps[:, 6 + h // 2, (h % 2) * DV:(h % 2 + 1) * DV], mixB[p][:, h * DV:(h + 1) * DV],
                                   ACT.Square, accum_out=msq[:, p, 1 + h:2 + h])
                last.then_inc(S["asm_stats"], 1)

            def mix_high(i, p):
                T = 2 * i + p
                for g in range(4):
                    act.wait_ge(S["asm_tr"], 4 * T + (g + 1))
                    act.activation(a_hi[:, 4 * g:4 * g + 4, bass.ds(T * P, P)], by_chunk(ps[:, g, :]), ACT.Copy)\
                        .then_inc(S["mixT_hi"], 1)

            def mix_pair(i, last):
                stats(i, 1)
                mix_high(i, 0)
                if not last:
                    stats(i + 1, 0)
                mix_high(i, 1)

            stats(0, 0)
            with act.Fori(0, TT // 2 - 1) as i:
                mix_pair(i, False)
            mix_pair(TT // 2 - 1, True)

            def evict_plain(b):
                for n in range(8):
                    act.wait_ge(S["bank_ready"], 8 * b + (n + 1))
                    act.wait_ge(S["stage_free"], 8 * b + (n - 3))
                    act.activation(stage[:, n % 4, :], ps[:, n, :], ACT.Copy).then_inc(S["bank_staged"], 1)

            with act.Fori(BLK, BLK + OBLK - 1) as b:
                for m in range(3, CPB):
                    high(b, m)
                for m in range(3):
                    high(b + 1, m)
                evict_plain(b)
            for m in range(3, CPB):
                high(BLK + OBLK - 1, m)
            evict_plain(BLK + OBLK - 1)

            def r_square(i, p):
                act.wait_ge(rxsem[p], 16 * i + 16)
                if not (isinstance(i, int) and i == 0 and p == 0):
                    act.wait_ge(S["r_sq"], 4 * i + p)
                act.activation(squares[:, :], rx[:, p, :], ACT.Square, accum_out=rsmall[:, p:p + 1]).then_inc(S["r_sq"], 1)

            def r_evict(T):
                if T:
                    act.wait_ge(S["r_logit"], T)
                for g in (0, 2):
                    act.wait_ge(S["r_tr"], 4 * T + (g + 1))
                    act.activation(flat2(rT[:, T % 2, 4 * g:4 * g + 4, :]), ps[:, TRBANK[(4 * T + g) % 6], :], ACT.Copy)\
                        .then_inc(S["r_tA"], 1)

            r_square(0, 0)
            r_square(0, 1)
            for T in range(TT):
                if T + 2 < TT:
                    r_square((T + 2) // 4, (T + 2) % 4)
                r_evict(T)
            act.wait_ge(S["r_logit"], TT + 1)
            for a in range(2):
                act.activation(affT[:, a * BW:(a + 1) * BW], ps[0:NE, 4 + a, :], ACT.Copy).then_inc(S["aff_out"], 1)
            act.wait_ge(S["smax"], 2)
            act.activation(affs[:, :, :], affs[:, :, :], ACT.Exp).then_inc(S["r_exp"], 1)
            for a in range(2):
                act.wait_ge(S["aff_tr"], a + 2)
                act.activation(affT[:, a * BW:(a + 1) * BW], ps[0:NE, a, :], ACT.Copy).then_inc(S["aff_out"], 1)

            def piece_high(e, j):
                slot = (j // 2) % (ERAW // 2)
                act.wait_ge(ersem[slot], 32 * (EPC // ERAW) * e + (32 * (j // ERAW + 1) + ER0[slot]))
                if j >= ESPL:
                    act.wait_ge(*used(e, j - ESPL))
                elif not (isinstance(e, int) and e == 0):
                    act.wait_ge(*used(e - 1, j + EPC - ESPL))
                act.activation(ehi[:, j % ESPL, :], eraw[:, j % ERAW, :], ACT.Copy).then_inc(S["e_hi"], 1)

            def x_high(e, g):
                act.wait_ge(S["xtr"], 4 * e + (g + 1))
                act.activation(flat2(xh[:, 4 * g:4 * g + 4, :]), ps[:, 6 + g % 2, :], ACT.Copy).then_inc(S["x_hi"], 1)

            def h_high(e, g):
                act.wait_ge(S["htr"], 2 * e + (g + 1))
                act.activation(flat2(hh[:, 4 * g:4 * g + 4, :]), ps[:, 4 + g, :], ACT.Copy).then_inc(S["h_hi"], 1)

            def expert(e, last):
                for j in range(ESPL, 30 + ESPL):
                    piece_high(e, j)
                act.wait_ge(S["gu_ready"], e + 1)
                for c in range(2):
                    act.activation(hact[:, c * BW:(c + 1) * BW], ps[:, c, :], ACT.Silu).then_inc(S["silu2"], 1)
                if last:
                    h_high(e, 0)
                    h_high(e, 1)
                else:
                    x_high(e + 1, 0)
                    x_high(e + 1, 1)
                    h_high(e, 0)
                    h_high(e, 1)
                    x_high(e + 1, 2)
                    x_high(e + 1, 3)
                for j in range(30 + ESPL, EPC):
                    piece_high(e, j)
                if not last:
                    for j in range(ESPL):
                        piece_high(e + 1, j)
                act.wait_ge(S["gcol_done"], e + 1)
                act.wait_ge(S["ey_free"], e + 1)
                for c in range(2):
                    act.wait_ge(S["y_ready"], 4 * e + (c + 1))
                    act.activation(ey[:, c * BW:(c + 1) * BW], ps[:, 4 + c, :], ACT.Copy, scale=gcol[:, 0:1]).then_inc(S["y_out"], 1)

            for j in range(ESPL):
                piece_high(0, j)
            for g in range(4):
                x_high(0, g)
            with act.Fori(0, NE - 1) as e:
                expert(e, False)
            expert(NE - 1, True)

            with act.Fori(TT // 4, TT // 2) as i:
                for p in range(4):
                    r_square(i, p)

        @block.vector
        def _(dve):
            step = Steps(dve, S["dve_step"])

            def low(b, m):
                dve.wait_ge(S["w_hi"], CPB * b + (m + 1))
                dve.tensor_tensor(wlo[:, m % RING, :], raw[:, m % RING, :], whi[:, m % RING, :].bitcast(F32), ALU.subtract)\
                    .then_inc(S["w_lo"], 1)

            dve.wait_ge(S["const_in"], 32)
            dve.wait_ge(S["wg_hi"], 1)
            dve.tensor_tensor(wg_lo[:, :], wg_raw[:, :], wg_hi[:, :].bitcast(F32), ALU.subtract).then_inc(S["wg_done"], 1)
            for k in range(KD):
                if k % 2 == 0 :
                    low(0, k // 2)
                dve.wait_ge(S["hT_hi"], k + 1)
                dve.scalar_tensor_tensor(out=a_lo[:, k, :], in0=(t0, t1)[k % 2][:, :], scalar=gmix[:, k:k + 1],
                                         in1=a_hi[:, k, :].bitcast(F32), op0=ALU.mult, op1=ALU.subtract).then_inc(S["hT_lo"], 1)
            for m in range(3):
                low(1, m)
            dve.wait_ge(S["xn_sq"], KD)
            ss = ssum[:, :].rearrange("p (t h) -> p t h", h=2)
            dve.tensor_tensor(meansq[:, :], ss[:, :, 0], ss[:, :, 1], ALU.add).then_inc(S["dve_step"], 1)
            step.settle()
            dve.tensor_scalar(meansq[:, :], meansq[:, :], 1.0 / D, EPS, ALU.mult, ALU.add).then_inc(S["meansq_done"], 1)
            with dve.Fori(1, ROWBLK) as b:
                for m in range(3, CPB):
                    low(b, m)
                for m in range(3):
                    low(b + 1, m)

            def bc(ap, n):
                return ap.unsqueeze(2).broadcast_to([ap.shape[0], ap.shape[1], n])

            low(ROWBLK, 3)
            dve.wait_ge(S["gates_ready"], 1)
            dve.wait_ge(S["rstd_bc_in"], 16)
            dve.tensor_tensor(t0[:, :], flat2(ps[:, 0:2, :]), rstd_bc[:, :], ALU.mult).then_inc(S["gates_copied"], 1)
            dve.wait_ge(S["gates_copied"], 1)
            dve.wait_ge(S["gpad_zero"], 1 + 4 + 4)
            dve.wait_ge(S["gb_in"], 64)
            for dst, rows in ((t1, slice(64, 128)), (t0, slice(0, 64))):
                dve.tensor_scalar(dst[0:64, :], t0[rows, :], g_bias[rows, 0:1], g_bias[rows, 1:2], ALU.mult, ALU.add)\
                    .then_inc(S["grows_out"], 1)
            T0, T1, T2, T3 = t0[0:64, :], t1[0:64, :], t2[0:64, 0:1024], t3[0:64, :]
            dve.wait_ge(S["grows_out"], 2)
            dve.scalar_tensor_tensor(out=T2, in0=T1, scalar=-1.0, in1=T1, op0=ALU.mult, op1=ALU.max).then_inc(S["gate_arg"], 1)
            dve.wait_ge(S["gate_act"], 1)
            dve.scalar_tensor_tensor(out=T1, in0=T1, scalar=0.0, in1=T2, op0=ALU.min, op1=ALU.subtract).then_inc(S["dve_step"], 1)
            step.settle()
            dve.wait_ge(S["mask_done"], 1)
            ways = ((slice(0, 4), 1), (slice(32, 36), -1))
            for r, way in ways:
                dve.tensor_tensor_scan(out=t1[r, ::way], data0=t3[r, :], data1=t1[r, ::way], initial=0.0,
                                       op0=ALU.mult, op1=ALU.add).then_inc(S["dve_step"], 1)
                step.settle()
            dve.tensor_tensor(T0, T0, T1, ALU.subtract).then_inc(S["dve_step"], 1)
            step.settle()
            dve.tensor_scalar(T3, T3, -1.0, -NEG, ALU.add, ALU.mult).then_inc(S["dve_step"], 1)
            step.settle()
            for r, way in ways:
                dve.tensor_tensor_scan(out=t2[r, 0:1024][:, ::way], data0=t3[r, :], data1=t0[r, ::way], initial=0.0,
                                       op0=ALU.add, op1=ALU.max).then_inc(S["dve_step"], 1)
                step.settle()
            low(ROWBLK, 4)
            T1n, T2n = T1.rearrange("p (n j) -> p n j", j=P), T2.rearrange("p (n j) -> p n j", j=P)
            T0n, T3n = T0.rearrange("p (n j) -> p n j", j=P), T3.rearrange("p (n j) -> p n j", j=P)
            for r, way in ways:
                e = P - 1 if way > 0 else 0
                dve.tensor_copy(b_last[r, :], T1n[r, :, e]).then_inc(S["dve_step"], 1)
                step.settle()
                dve.tensor_copy(c_last[r, :], T2n[r, :, e]).then_inc(S["dve_step"], 1)
                step.settle()
            for r, way in ways:
                dve.tensor_tensor_scan(out=m_next[r, 1:TT + 1][:, ::way], data0=c_last[r, ::way], data1=b_last[r, ::way],
                                       initial=0.0, op0=ALU.max, op1=ALU.add).then_inc(S["dve_step"], 1)
                step.settle()
                at = 0 if way > 0 else 2
                dve.tensor_copy(m_prev[r, :], m_next[r, at:at + TT]).then_inc(S["dve_step"], 1)
                step.settle()
            dve.tensor_tensor(m_end[:, :], m_prev[:, :], c_last[:, :], ALU.max).then_inc(S["dve_step"], 1)
            step.settle()
            dve.tensor_tensor(decay[:, :], m_prev[:, :], m_end[:, :], ALU.subtract).then_inc(S["gate_arg"], 1)
            low(ROWBLK, 5)
            dve.tensor_tensor(T2n, T2n, bc(m_prev[:, :], P), ALU.max).then_inc(S["dve_step"], 1)
            step.settle()
            dve.tensor_tensor(T3, T1, T2, ALU.add).then_inc(S["gate_arg"], 1)
            dve.tensor_scalar(T0, T0, LNS, None, ALU.add).then_inc(S["dve_step"], 1)
            step.settle()
            dve.wait_ge(S["gate_act"], 3)
            dve.tensor_tensor(T3n, T0n, bc(m_end[:, :], P), ALU.subtract).then_inc(S["gate_arg"], 1)
            dve.wait_ge(S["gate_act"], 4)
            dve.tensor_tensor(T3n, bc(m_prev[:, :], P), T2n, ALU.subtract).then_inc(S["gate_arg"], 1)
            dve.wait_ge(S["acc_free"], 1)
            dve.memset(t2[:, 0:2], 0.0).then_inc(S["dve_step"], 1)
            step.settle()
            dve.memset(t2[:, 1026:1028], 0.0).then_inc(S["conv_free"], 1)

            def evict_feats(b):
                for n in range(8):
                    dve.wait_ge(S["bank_ready"], 8 * b + (n + 1))
                    dve.wait_ge(S["stage_free"], 8 * b + (n - 3))
                    dve.tensor_tensor(stage[:, n % 4, :], ps[:, n, :], rstd_bc[:, (n % 2) * BW:(n % 2 + 1) * BW], ALU.mult)\
                        .then_inc(S["bank_staged"], 1)

            dve.wait_ge(S["rstd_bc_in"], 16)
            dve.wait_ge(S["gate_act"], 5)
            for m in range(6, CPB):
                low(ROWBLK, m)
            for b in (ROWBLK, ROWBLK + 1):
                for m in range(3):
                    low(b + 1, m)
                evict_feats(b)
                if b == ROWBLK:
                    for m in range(3, CPB):
                        low(b + 1, m)
            with dve.Fori(ROWBLK + 2, BLK) as b:
                step.enter(b - (ROWBLK + 2), 2 * (CONVW - 1))
                for m in range(3, CPB):
                    low(b, m)
                    if m in (4, 6):
                        q = (m - 4) // 2
                        c = 2 * b + (q - 2 * (ROWBLK + 2))
                        dve.wait_ge(S["conv_in"], 32 * c + 32)
                        dve.wait_ge(S["acc_free"], c + 1)
                        dve.tensor_scalar(t0[:, :], t2[:, 0:1024], cw[:, q, 0:1], None, ALU.mult).then_inc(S["dve_step"], 1)
                        step.settle()
                        for j in range(1, CONVW):
                            last = dve.scalar_tensor_tensor(out=t0[:, :], in0=t2[:, j:j + 1024], scalar=cw[:, q, j:j + 1],
                                                            in1=t0[:, :], op0=ALU.mult, op1=ALU.add)
                            if j < CONVW - 1:
                                last.then_inc(S["dve_step"], 1)
                                step.settle()
                            else:
                                last.then_inc(S["conv_free"], 1)
                for m in range(3):
                    low(b + 1, m)
                evict_feats(b)
                step.leave(BLK - ROWBLK - 2)

            dve.sem_inc(S["scored"], 2)
            dve.sem_inc(S["na_out_done"], 2)

            def score(i, u):
                hb, p, w = u // 8, u % 8, WIDE[u % 8]
                if u % 8 == 0:
                    dve.wait_ge(S["bias_ready"], 4 * i + (2 * hb + 2))
                dve.wait_ge(S["qk_done"], 16 * i + (u + 1))
                dve.wait_ge(S["transposed"], 16 * i + (u + 1))
                dve.sem_inc(S["dve_past"], 1)
                b = flat2(bias9[:, hb, :, :]) if w > 8 * GW else flat2(bias[:, hb, BROW[p] - 1:BROW[p] + 7, :])
                dve.tensor_tensor_reduce(out=prob[:, u % 2, 0:w], in0=SC[u % 2][:, 0:w], in1=b, scale=1.0, scalar=3 * NEG,
                                         op0=ALU.add, op1=ALU.max, accum_out=top[:, u % 2:u % 2 + 1]).then_inc(S["scored"], 1)
                dve.wait_ge(S["scored"], 16 * i + (u + 3))
                dve.tensor_scalar(ntop[:, u % 2:u % 2 + 1], top[:, u % 2:u % 2 + 1], -1.0, None, ALU.mult).then_inc(S["na_max"], 1)

            def finish(i, u):
                dve.wait_ge(S["exp_done"], 16 * i + (u + 1))
                dve.reciprocal(pinv[:, u % 2:u % 2 + 1], psumr[:, u % 4:u % 4 + 1]).then_inc(S["na_step"], 1)
                dve.wait_ge(S["na_step"], 16 * i + (u + 1))
                dve.wait_ge(S["pv_done"], 16 * i + (u + 3))
                dve.tensor_scalar(na_out[:, u % 8, bass.ds((2 * i + u // 8) * HD, HD)], ps[:, 6 + u % 2, 0:HD],
                                  pinv[:, u % 2:u % 2 + 1], None, ALU.mult).then_inc(S["na_out_done"], 1)

            def na_pair(i, last):
                for u in range(16):
                    if u < 14:
                        score(i, u + 2)
                    elif not last:
                        score(i + 1, u - 14)
                    finish(i, u)

            score(0, 0)
            score(0, 1)
            dve.wait_ge(S["cols_ready"], 1)
            for q in range(4):
                src = ps[:, 4 + 2 * (q // 2):6 + 2 * (q // 2), :].rearrange("p a (n r) -> p (a n) r", r=P)
                src = src[:, :, 64 * (q % 2):64 * (q % 2) + 64].rearrange("p n (d h) -> p n d h", d=2)[:, :, :, 0:MLH]
                dve.tensor_copy(cols[:, :, q, :, :], src).then_inc(S["cols_out"], 1)
            with dve.Fori(0, NAH // 2 - 1) as i:
                na_pair(i, False)
            na_pair(NAH // 2 - 1, True)

            dve.wait_ge(S["gates_in"], 32)
            dve.sem_inc(S["qkw_done"], 2)
            dve.sem_inc(S["c_updated"], 2)
            dve.sem_inc(S["hs_done"], 2)
            with dve.Fori(0, MLH // 2) as i:
                step.enter(i, 2 * 3)
                for hb in range(2):
                    h = 2 * i + hb
                    dve.wait_ge(S["c_updated"], 16 * h + 2)
                    dve.wait_ge(S["cols_out"], 4)
                    dve.memset(cst[:, :, :], 0.0).then_inc(S["c_zeroed"], 1)
                    dve.tensor_copy(hcols[:, hb, :, :, :],
                                    cols[:, :, :, :, bass.ds(h, 1)].rearrange("p n q d h -> p n q (d h)")).then_inc(S["hcols_ready"], 1)
                    dve.tensor_copy(hdec[:, hb, :, :],
                                    decbc[:, :, bass.ds(h, 1), :].rearrange("p d h n -> p (d h) n")).then_inc(S["hcols_ready"], 1)
                    dve.wait_ge(S["kn_ready"], h + 1)
                    dve.wait_ge(S["kw_done"], 16 * h + 1)
                    for j in range(2):
                        dve.tensor_copy(flat2(kn[:, 4 * j:4 * j + 4, :]), ps[:, j, :]).then_inc(S["kn_out"], 1)

                    def weigh(u):
                        n, d = ml_unit(u)
                        dve.wait_ge(S["masked"], 16 * h + (u + 1))
                        dve.wait_ge(S["num_done"], 16 * h + (u + 1))
                        dve.tensor_tensor(qkw[:, u % 2, :], st[:, n * P:(n + 1) * P], wexp[:, u % 2, :], ALU.mult)\
                            .then_inc(S["qkw_done"], 1)

                    dve.wait_ge(S["st_out"], 2 * h + 2)
                    weigh(0)
                    dve.wait_ge(S["hcols_ready"], 2 * h + 2)
                    for u in range(16):
                        n, d = ml_unit(u)
                        if u < 15:
                            weigh(u + 1)
                        if u < 2:
                            dve.wait_ge(S["c_zeroed"], h + 1)
                        else:
                            dve.wait_ge(S["c_updated"], 16 * h + (u + 1))
                        dve.wait_ge(S["kv_done"], 16 * h + (u + 3))
                        dve.wait_ge(S["intr_done"], 16 * h + (u + 1))
                        dve.scalar_tensor_tensor(out=cst[:, d, :], in0=cst[:, d, :], scalar=hdec[:, hb, d, n:n + 1],
                                                 in1=ps[:, 2 + u % 2, 0:DV + 1], op0=ALU.mult, op1=ALU.add).then_inc(S["c_updated"], 1)
                        dve.wait_ge(S["num_done"], 16 * h + (u + 3))
                        dve.wait_ge(S["t_done"], 16 * h + (u + 3))
                        dve.tensor_tensor(hall[:, n, d, :], ps[:, 4 + u % 2, 0:DV + 1], inter[:, u % 2, :], ALU.add)\
                            .then_inc(S["hs_done"], 1)
                    dve.wait_ge(S["hs_done"], 16 * h + (16 + 2))
                    s1 = hall[:, :, :, DV]
                    dve.scalar_tensor_tensor(out=den[:, :, :], in0=s1, scalar=-1.0, in1=s1, op0=ALU.mult, op1=ALU.max)\
                        .then_inc(S["dve_step"], 1)
                    step.settle()
                    dve.tensor_tensor(den[:, :, :], den[:, :, :], hcols[:, hb, :, 3, :], ALU.max).then_inc(S["dve_step"], 1)
                    step.settle()
                    dve.reciprocal(den[:, :, :], den[:, :, :]).then_inc(S["den_done"], 1)
                    for n in range(TT):
                        dve.wait_ge(S["fwd_out"], 8 * h + (n + 1))
                        last = dve.scalar_tensor_tensor(out=mh[:, hb, n, :], in0=hall[:, n, 1, 0:DV], scalar=den[:, n, 1:2],
                                                        in1=mh[:, hb, n, :], op0=ALU.mult, op1=ALU.add)
                    last.then_inc(S["dve_step"], 1)
                    step.settle()
                    dve.sem_inc(S["ml_head_done"], 1)
                step.leave(MLH // 2)

            dve.wait_ge(S["mh_free"], 2 + MLH)
            dve.sem_inc(S["mixT_lo"], 4)

            def scale_mix(i, p):
                T = 2 * i + p
                dve.wait_ge(S["asm_stats"], T + 1)
                dve.tensor_scalar(msq[:, p, 0:1], msq[:, p, 0:1], 1.0 / (NAH * HD), EPS, ALU.mult, ALU.add)
                dve.tensor_scalar(msq[:, p, 1:5], msq[:, p, 1:5], 1.0 / DV, EPS, ALU.mult, ALU.add).then_inc(S["asm_mean"], 1)
                dve.wait_ge(S["rs_done"], T + 1)
                dve.wait_ge(S["asm_gate"], T + 1)
                dve.scalar_tensor_tensor(out=mixA[p], in0=mixA[p], scalar=rs[:, p, 0:1], in1=gain_na[:, :],
                                         op0=ALU.mult, op1=ALU.mult)
                for h in range(MLH):
                    at = slice(h * DV, (h + 1) * DV)
                    last = dve.scalar_tensor_tensor(out=mixB[p][:, at], in0=mixB[p][:, at], scalar=rs[:, p, 1 + h:2 + h],
                                                    in1=mixO[p][:, at], op0=ALU.mult, op1=ALU.mult)
                last.then_inc(S["asm_scaled"], 1)

            def mix_low(i, p):
                T = 2 * i + p
                for g in range(4):
                    dve.wait_ge(S["mixT_hi"], 4 * T + (g + 1))
                    four = (slice(None), slice(4 * g, 4 * g + 4), bass.ds(T * P, P))
                    dve.tensor_tensor(a_lo[four], by_chunk(ps[:, g, :]), a_hi[four].bitcast(F32), ALU.subtract)\
                        .then_inc(S["mixT_lo"], 1)

            def mix_pair(i, last):
                scale_mix(i, 1)
                mix_low(i, 0)
                if not last:
                    scale_mix(i + 1, 0)
                mix_low(i, 1)

            scale_mix(0, 0)
            with dve.Fori(0, TT // 2 - 1) as i:
                mix_pair(i, False)
            mix_pair(TT // 2 - 1, True)

            with dve.Fori(BLK, BLK + OBLK - 1) as b:
                for m in range(3, CPB):
                    low(b, m)
                for m in range(3):
                    low(b + 1, m)
            for m in range(3, CPB):
                low(BLK + OBLK - 1, m)

            dve.wait_ge(S["rc_in"], 32)

            def r_mean(i, p):
                dve.wait_ge(S["r_sq"], 4 * i + (p + 1))
                dve.tensor_scalar(rsmall[:, 4 + p:5 + p], rsmall[:, p:p + 1], 1.0 / D, EPS, ALU.mult, ALU.add).then_inc(S["r_mean"], 1)

            def r_normal(i, p):
                dve.wait_ge(S["r_rstd"], 4 * i + (p + 1))
                if isinstance(i, int) and i < 2 and 4 * i + p >= 2:
                    dve.wait_ge(S["r_tr"], 4 * (4 * i + p - 1))
                dve.wait_ge(S["rh_free"], 4 * i + (p + 1))
                dve.scalar_tensor_tensor(out=rh[:, p % 2, :], in0=rx[:, p, :], scalar=rstd[:, p:p + 1], in1=gbc[:, :],
                                         op0=ALU.mult, op1=ALU.mult).then_inc(S["r_norm"], 1)

            def r_evict(T):
                if T:
                    dve.wait_ge(S["r_logit"], T)
                for g in (1, 3):
                    dve.wait_ge(S["r_tr"], 4 * T + (g + 1))
                    dve.tensor_copy(flat2(rT[:, T % 2, 4 * g:4 * g + 4, :]), ps[:, TRBANK[(4 * T + g) % 6], :]).then_inc(S["r_tD"], 1)

            r_mean(0, 0)
            r_mean(0, 1)
            r_normal(0, 0)
            for T in range(TT):
                if T + 2 < TT:
                    r_mean((T + 2) // 4, (T + 2) % 4)
                if T + 1 < TT:
                    r_normal((T + 1) // 4, (T + 1) % 4)
                r_evict(T)
            lg = ps[:, 6, 0:TT * NE].rearrange("p (t e) -> p t e", e=NE)
            dve.wait_ge(S["aff_tr"], 1)
            dve.tensor_reduce(out=smx[:, :], in_=lg, axis=AX.X, op=ALU.max).then_inc(S["smax"], 1)
            dve.wait_ge(S["smax"], 1)
            dve.tensor_tensor(affs[:, :, :], lg, bc(smx[:, :], NE), ALU.subtract).then_inc(S["smax"], 1)
            dve.wait_ge(S["r_exp"], 1)
            dve.tensor_reduce(out=smx[:, :], in_=affs[:, :, :], axis=AX.X, op=ALU.add).then_inc(S["dve_step"], 1)
            step.settle()
            dve.reciprocal(smx[:, :], smx[:, :]).then_inc(S["dve_step"], 1)
            step.settle()
            dve.tensor_tensor(affs[:, :, :], affs[:, :, :], bc(smx[:, :], NE), ALU.mult).then_inc(S["affn"], 1)
            dve.wait_ge(S["aff_out"], 4)
            for r in range(TOPR):
                at = slice(8 * r, 8 * r + 8)
                dve.max(best[:, at], affT[:, :]).then_inc(S["dve_step"], 1)
                step.settle()
                dve.max_index(besti[:, at], best[:, at], affT[:, :]).then_inc(S["dve_step"], 1)
                step.settle()
                if r < TOPR - 1:
                    dve.match_replace(out=affT[:, :], in_to_replace=best[:, at], in_values=affT[:, :], imm_value=-1.0)\
                        .then_inc(S["dve_step"], 1)
                    step.settle()
            dve.tensor_copy(bestf[:, :], besti[:, :]).then_inc(S["affn"], 1)
            dve.wait_ge(S["aff_tr"], 4)
            dve.tensor_copy(gateT[:, :], ps[:, 0, 0:NE]).then_inc(S["best_out"], 1)
            dve.tensor_copy(tokT[:, :], ps[:, 0, NE:2 * NE]).then_inc(S["best_out"], 1)

            def piece_low(e, j):
                dve.wait_ge(S["e_hi"], EPC * e + (j + 1))
                dve.tensor_tensor(elo[:, j % ESPL, :], eraw[:, j % ERAW, :], ehi[:, j % ESPL, :].bitcast(F32), ALU.subtract)\
                    .then_inc(S["e_lo"], 1)

            def x_low(e, g):
                dve.wait_ge(S["x_hi"], 4 * e + (g + 1))
                dve.tensor_tensor(flat2(xl[:, 4 * g:4 * g + 4, :]), ps[:, 6 + g % 2, :],
                                  flat2(xh[:, 4 * g:4 * g + 4, :]).bitcast(F32), ALU.subtract).then_inc(S["x_lo"], 1)

            def h_low(e, g):
                dve.wait_ge(S["h_hi"], 2 * e + (g + 1))
                dve.tensor_tensor(flat2(hl[:, 4 * g:4 * g + 4, :]), ps[:, 4 + g, :],
                                  flat2(hh[:, 4 * g:4 * g + 4, :]).bitcast(F32), ALU.subtract).then_inc(S["h_lo"], 1)

            def expert(e, last):
                for j in range(ESPL, 30 + ESPL):
                    piece_low(e, j)
                for c in range(2):
                    dve.wait_ge(S["silu2"], 2 * e + (c + 1))
                    dve.tensor_tensor(hact[:, c * BW:(c + 1) * BW], ps[:, 2 + c, :], hact[:, c * BW:(c + 1) * BW], ALU.mult)\
                        .then_inc(S["hmul"], 1)
                if last:
                    h_low(e, 0)
                    h_low(e, 1)
                else:
                    x_low(e + 1, 0)
                    x_low(e + 1, 1)
                    h_low(e, 0)
                    h_low(e, 1)
                    x_low(e + 1, 2)
                    x_low(e + 1, 3)
                for j in range(30 + ESPL, EPC):
                    piece_low(e, j)
                if not last:
                    for j in range(ESPL):
                        piece_low(e + 1, j)
                dve.wait_ge(S["gcol_done"], e + 1)
                dve.wait_ge(S["ey_free"], e + 1)
                for c in range(2, 4):
                    dve.wait_ge(S["y_ready"], 4 * e + (c + 1))
                    dve.tensor_scalar(ey[:, c * BW:(c + 1) * BW], ps[:, 4 + c, :], gcol[:, 0:1], None, ALU.mult).then_inc(S["y_out"], 1)

            for j in range(ESPL):
                piece_low(0, j)
            for g in range(4):
                x_low(0, g)
            with dve.Fori(0, NE - 1) as e:
                expert(e, False)
            expert(NE - 1, True)

            dve.wait_ge(S["rc_in"], 48)
            with dve.Fori(TT // 4, TT // 2) as i:
                for p in range(4):
                    r_mean(i, p)
                    r_normal(i, p)

        @block.tensor
        def _(pe):
            def rows_block(b, src_hi, src_lo, first=False, bank_wait=True):
                for k in range(KD):
                    m = k // 2
                    if k % 2 == 0:
                        pe.wait_ge(S["w_lo"], CPB * b + (m + 1))
                    if first:
                        pe.wait_ge(S["hT_lo"], k + 1)
                    hi = whi[:, m % RING, (k % 2) * BW:(k % 2 + 1) * BW]
                    lo = wlo[:, m % RING, (k % 2) * BW:(k % 2 + 1) * BW]
                    for n in range(TT):
                        if k == 0 and bank_wait:
                            pe.wait_ge(S["bank_staged"], 8 * b + (n - 7))
                        xs = src_hi[:, k, n * P:(n + 1) * P]
                        pe.matmul(ps[:, n, :], xs, hi, start=(k == 0), stop=False)
                        pe.matmul(ps[:, n, :], xs, lo, start=False, stop=False)
                        last = pe.matmul(ps[:, n, :], src_lo[:, k, n * P:(n + 1) * P], hi, start=False, stop=(k == KD - 1))
                        if k == KD - 1:
                            last.then_inc(S["bank_ready"], 1)
                    if k % 2 == 1 and k < KD - 1:
                        last.then_inc(S["w_used"], 1)

            def feats_block(b, bank_wait=True):
                for k in range(KD):
                    m = k // 2
                    if k % 2 == 0:
                        pe.wait_ge(S["w_lo"], CPB * b + (m + 1))
                    for g in range(4):
                        at = (k % 2) * BW + g * P
                        hi, lo = whi[:, m % RING, at:at + P], wlo[:, m % RING, at:at + P]
                        for w, src in ((hi, a_hi), (hi, a_lo), (lo, a_hi)):
                            for h in range(2):
                                n = 2 * g + h
                                if k == 0 and w is hi and src is a_hi and bank_wait:
                                    pe.wait_ge(S["bank_staged"], 8 * b + (n - 7))
                                last = pe.matmul(ps[:, n, :], w, src[:, k, h * BW:(h + 1) * BW],
                                                 start=(k == 0 and w is hi and src is a_hi),
                                                 stop=(k == KD - 1 and w is lo))
                                if k == KD - 1 and w is lo:
                                    last.then_inc(S["bank_ready"], 1)
                    if k % 2 == 1 and k < KD - 1:
                        last.then_inc(S["w_used"], 1)

            rows_block(0, a_hi, a_lo, first=True, bank_wait=False)
            with pe.Fori(1, ROWBLK) as b:
                rows_block(b, a_hi, a_lo)
            pe.wait_ge(S["bank_staged"], 8 * ROWBLK)
            pe.wait_ge(S["wg_done"], 1)
            for k in range(KD):
                for w, a in ((wg_hi, a_hi), (wg_lo, a_hi), (wg_hi, a_lo)):
                    at = P * (k // 8) + 4 * (k % 8)
                    window = w[:, at:at + P]
                    for c in range(2):
                        last = pe.matmul(ps[:, c, :], window, a[:, k, c * BW:(c + 1) * BW], start=(k == 0 and a is a_hi and w is wg_hi),
                                         stop=(k == KD - 1 and a is a_lo))
            last.then_inc(S["gates_ready"], 1)
            pe.wait_ge(S["gates_copied"], 1)
            with pe.Fori(ROWBLK, BLK) as b:
                feats_block(b)

            pe.wait_ge(S["ident_done"], 1)
            pe.wait_ge(S["bank_staged"], 8 * BLK)
            pe.sem_inc(S["transposed"], 2)
            pe.sem_inc(S["pv_done"], 2)

            def qk(i, u):
                hb, p, w = u // 8, u % 8, WIDE[u % 8]
                if p == 0:
                    pe.wait_ge(S["q_scaled"], 2 * i + (hb + 1))
                    pe.wait_ge(nkvsem[hb], 32 * i + 32)
                pe.wait_ge(S["scored"], 16 * i + (u + 1))
                q, k0 = naq[:, hb, p * P:(p + 1) * P], KEY0[p] * P
                last = pe.matmul(SC[u % 2][:, 0:BW], q, nak[:, hb, k0:k0 + BW], start=True, stop=True)
                if w > BW:
                    last = pe.matmul(SC[u % 2][:, BW:w], q, nak[:, hb, k0 + BW:k0 + w], start=True, stop=True)
                last.then_inc(S["qk_done"], 1)

            def tr(i, u):
                pe.wait_ge(S["exp_done"], 16 * i + (u + 1))
                pe.wait_ge(S["pt_evicted"], 16 * i + (u + 1))
                for j in range(4):
                    last = pe.transpose(PTP[:, j * P:(j + 1) * P], prob[:, u % 2, j * P:(j + 1) * P], ident[:, :])
                if WIDE[u % 8] > 4 * P:
                    last = pe.transpose(PTP[0:GW, 4 * P:5 * P], prob[:, u % 2, 4 * P:4 * P + GW], ident[:, :])
                last.then_inc(S["transposed"], 1)

            def pv(i, u):
                hb, p = u // 8, u % 8
                pe.wait_ge(S["pt_evicted"], 16 * i + (u + 2))
                pe.wait_ge(S["na_out_done"], 16 * i + (u + 1))
                nk = 5 if WIDE[p] > 4 * P else 4
                for j in range(nk):
                    r = P if j < 4 else GW
                    last = pe.matmul(ps[:, 6 + u % 2, 0:HD], probT[0:r, u % 2, j, :], nav[0:r, hb, KEY0[p] + j, :],
                                     start=(j == 0), stop=(j == nk - 1))
                last.then_inc(S["pv_done"], 1)

            def na_pair(i, last):
                for u in range(16):
                    tr(i, u)
                    if u < 14:
                        qk(i, u + 2)
                    elif not last:
                        qk(i + 1, u - 14)
                    pv(i, u)

            qk(0, 0)
            qk(0, 1)
            pe.wait_ge(S["gates_in"], 32)
            for a in range(2):
                for n in range(TT):
                    last = pe.transpose(ps[:, 4 + 2 * a + n // 4, (n % 4) * P:(n % 4 + 1) * P], qrows[:, a, n * P:(n + 1) * P], ident[:, :])
            last.then_inc(S["cols_ready"], 1)
            pe.wait_ge(S["cols_out"], 4)
            with pe.Fori(0, NAH // 2 - 1) as i:
                na_pair(i, False)
            na_pair(NAH // 2 - 1, True)

            pe.sem_inc(S["kv_done"], 2)
            pe.sem_inc(S["num_done"], 2)
            pe.wait_ge(S["scored"], 64 + 2)
            pe.wait_ge(S["na_out_done"], 64 + 2)
            pe.wait_ge(S["pt_evicted"], 64 + 1)
            pe.wait_ge(S["ones_done"], 2)
            with pe.Fori(0, MLH // 2) as i:
                for hb in range(2):
                    h = 2 * i + hb
                    pe.wait_ge(mlsem[hb], 80 * i + 80)
                    for n in range(TT):
                        last = pe.transpose(ps[:, n // 4, (n % 4) * P:(n % 4 + 1) * P], mk[:, hb, n * P:(n + 1) * P], ident[:, :])
                    last.then_inc(S["kn_ready"], 1)
                    pe.wait_ge(S["hs_done"], 16 * h + 2)
                    for n in range(TT):
                        last = pe.matmul(ps[:, 4 + n // 4, (n % 4) * P:(n % 4 + 1) * P], mk[:, hb, n * P:(n + 1) * P],
                                         mq[:, hb, n * P:(n + 1) * P], start=True, stop=True)
                    last.then_inc(S["st_ready"], 1)
                    pe.wait_ge(S["c_zeroed"], h + 1)
                    for u in range(16):
                        n, d = ml_unit(u)
                        pe.wait_ge(S["c_updated"], 16 * h + (u + 1))
                        pe.wait_ge(S["t_done"], 16 * h + (u + 1))
                        pe.matmul(ps[:, 6 + u % 2, 0:DV + 1], mq[:, hb, n * P:(n + 1) * P], cst[:, d, :],
                                  start=True, stop=True).then_inc(S["intr_done"], 1)
                        pe.wait_ge(S["kw_done"], 16 * h + (u + 2))
                        pe.matmul(ps[:, 2 + u % 2, 0:DV + 1], kw[:, u % 2, :], mv[:, hb, n, :],
                                  start=True, stop=True).then_inc(S["kv_done"], 1)
                        pe.wait_ge(S["qkw_done"], 16 * h + (u + 3))
                        pe.wait_ge(S["hs_done"], 16 * h + (u + 1))
                        pe.matmul(ps[:, 4 + u % 2, 0:DV + 1], qkw[:, u % 2, :], mv[:, hb, n, :],
                                  start=True, stop=True).then_inc(S["num_done"], 1)

            pe.wait_ge(S["st_out"], 2 * MLH)
            pe.wait_ge(S["hs_done"], 64 + 2)
            with pe.Fori(0, TT // 2) as i:
                for p in range(2):
                    T = 2 * i + p
                    pe.wait_ge(S["asm_scaled"], T + 1)
                    for g in range(4):
                        pe.wait_ge(S["mixT_lo"], 4 * T + (g + 1))
                        src = mixA[p] if g < 2 else mixB[p]
                        for j in range(4):
                            at = (4 * (g % 2) + j) * P
                            last = pe.transpose(ps[:, g, j * P:(j + 1) * P], src[:, at:at + P], ident[:, :])
                        last.then_inc(S["asm_tr"], 1)

            pe.wait_ge(S["mixT_lo"], 4 + 4 * TT)
            with pe.Fori(BLK, BLK + OBLK) as b:
                rows_block(b, a_hi, a_lo)

            pe.wait_ge(S["bank_staged"], 8 * (BLK + OBLK))
            pe.wait_ge(S["rc_in"], 32)
            pe.sem_inc(S["r_logit"], 1)

            def r_transpose(T):
                pe.wait_ge(S["r_norm"], T + 1)
                for g in range(4):
                    before = 4 * T + g - 6
                    if before >= 0:
                        pe.wait_ge(S["r_tD"] if before % 2 else S["r_tA"], before // 2 + 1)
                    for j in range(4):
                        k = 4 * g + j
                        last = pe.transpose(ps[:, TRBANK[(4 * T + g) % 6], j * P:(j + 1) * P], rh[:, T % 2, k * P:(k + 1) * P], ident[:, :])
                    last.then_inc(S["r_tr"], 1)

            r_transpose(0)
            for T in range(TT):
                if T + 1 < TT:
                    r_transpose(T + 1)
                pe.wait_ge(S["r_tA"], 2 * T + 2)
                pe.wait_ge(S["r_tD"], 2 * T + 2)
                for k in range(KD):
                    last = pe.matmul(ps[0:NE, 4 + T // 4, (T % 4) * P:(T % 4 + 1) * P], wr[:, k, :], rT[:, T % 2, k, :],
                                     start=(k == 0), stop=(k == KD - 1), skip_group_check=True)
                last.then_inc(S["r_logit"], 1)
            pe.wait_ge(S["aff_out"], 2)
            for n in range(TT):
                last = pe.transpose(ps[:, 6, n * NE:(n + 1) * NE], affT[:, n * P:(n + 1) * P], ident[0:NE, 0:NE])
            last.then_inc(S["aff_tr"], 1)
            pe.wait_ge(S["affn"], 1)
            for n in range(TT):
                last = pe.transpose(ps[0:NE, n // 4, (n % 4) * P:(n % 4 + 1) * P], affs[:, n, :], ident[:, :])
                if n % 4 == 3:
                    last.then_inc(S["aff_tr"], 1)
            pe.wait_ge(S["aff_out"], 4)
            pe.wait_ge(S["affn"], 2)
            pe.transpose(ps[:, 0, 0:NE], best[:, :], ident[0:NE, 0:NE])
            pe.transpose(ps[:, 0, NE:2 * NE], bestf[:, :], ident[0:NE, 0:NE]).then_inc(S["aff_tr"], 1)

            def xt(e, g):
                if g >= 2:
                    pe.wait_ge(S["x_lo"], 4 * e + (g - 1))
                for j in range(4):
                    k = 4 * g + j
                    last = pe.transpose(ps[:, 6 + g % 2, j * P:(j + 1) * P], xg[:, k * P:(k + 1) * P], ident[:, :])
                last.then_inc(S["xtr"], 1)

            def ht(e, g):
                pe.wait_ge(S["hmul"], 2 * e + (g + 1))
                for j in range(4):
                    k = 4 * g + j
                    last = pe.transpose(ps[:, 4 + g, j * P:(j + 1) * P], hact[:, k * P:(k + 1) * P], ident[:, :])
                last.then_inc(S["htr"], 1)

            def expert(e, last_one):
                pe.wait_ge(S["x_lo"], 4 * e + 4)
                for k in range(KD):
                    pe.wait_ge(S["e_lo"], EPC * e + (2 * k + 2))
                    for a, parts in ((xh, (ehi, elo)), (xl, (ehi,))):
                        for j in range(2):
                            for c in range(2):
                                for w in parts:
                                    last = pe.matmul(ps[:, 2 * j + c, :], a[:, k, :], w[:, (2 * k + j) % ESPL, c * BW:(c + 1) * BW],
                                                     start=(k == 0 and a is xh and w is ehi), stop=(k == KD - 1 and a is xl))
                    if k < KD - 1:
                        last.then_inc(S["e_used"], 2)
                    else:
                        last.then_inc(S["gu_ready"], 1)
                pe.wait_ge(S["y_out"], 4 * e + 4)
                if not last_one:
                    pe.wait_ge(S["gathered"], 16 * e + 32)
                    xt(e + 1, 0)
                    xt(e + 1, 1)
                ht(e, 0)
                ht(e, 1)
                if not last_one:
                    xt(e + 1, 2)
                    xt(e + 1, 3)
                for k in range(KE):
                    if k % 4 == 0:
                        pe.wait_ge(S["h_lo"], 2 * e + (k // 4 + 1))
                    if k == 0:
                        pe.wait_ge(S["h_lo"], 2 * e + 2)
                        if not last_one:
                            pe.wait_ge(S["x_lo"], 4 * e + 8)
                    j0 = 2 * KD + 2 * k
                    pe.wait_ge(S["e_lo"], EPC * e + (j0 + 2))
                    for c in range(4):
                        sl = (j0 + c // 2) % ESPL
                        at = slice((c % 2) * BW, (c % 2 + 1) * BW)
                        pe.matmul(ps[:, 4 + c, :], hh[:, k, :], ehi[:, sl, at], start=(k == 0), stop=False)
                        pe.matmul(ps[:, 4 + c, :], hh[:, k, :], elo[:, sl, at], start=False, stop=False)
                        last = pe.matmul(ps[:, 4 + c, :], hl[:, k, :], ehi[:, sl, at], start=False, stop=(k == KE - 1))
                        if k == KE - 1:
                            last.then_inc(S["y_ready"], 1)
                    if k < KE - 1:
                        last.then_inc(S["e_used"], 2)

            pe.wait_ge(S["best_out"], 2)
            pe.sem_inc(S["y_out"], 4)
            pe.wait_ge(S["gathered"], 16)
            for g in range(4):
                xt(0, g)
            with pe.Fori(0, NE - 1) as e:
                expert(e, False)
            expert(NE - 1, True)


SCRATCH = {
    "rstd_d": (SEQ,), "x1": (SEQ, D), "rows": (SEQ, 3 * 1024), "feats": (24, P, SEQ), "conv": (8, P, SEQ),
    "m_rows": (8, SEQ), "decays": (8, TT), "q_rows": (2, P, SEQ), "na": (SEQ, 1024), "ml": (SEQ, 1024),
    "rpb_rep": (NAH, 15, GW, 127), "h2": (SEQ, D),
}


def kernel(x, norm_mix_g, w_in, b_gates, conv_w, conv_b, na_rpb, na_norm_g, ml_norm_g,
           w_out, norm_ffn_g, w_router, w_gate, w_up, w_down, final_norm_g):
    import concourse.bacc as bacc
    from concourse.bass_utils import run_bass_kernel_spmd

    w = w_in[0]
    cols_ = [w[:, 2048:3072], w[:, 4096:6144], w[:, 3072:4096], w[:, 0:2048]]
    w_mix = np.concatenate(cols_, axis=1).reshape(CPB, 2, P, BLK, BW).transpose(3, 0, 2, 1, 4)
    w_o = w_out[0].reshape(CPB, 2, P, OBLK, BW).transpose(3, 0, 2, 1, 4)
    ins = {
        "x": x[0], "xT": x[0].T,
        "w_stream": np.concatenate([w_mix, w_o], axis=0).reshape((BLK + OBLK) * CPB, P, 1024),
        "w_gates": w[:, 6144:6160].reshape(2, 8, P, 2, 2, MLH).transpose(2, 0, 4, 3, 1, 5).reshape(P, KD * 16),
        "g_mix": norm_mix_g[0].reshape(KD, P).T, "b_gates": b_gates[0],
        "conv_wb": np.concatenate([conv_w[0], conv_b], axis=0).reshape(CONVW + 1, 8, P).transpose(1, 2, 0),
        "rpb": na_rpb[0], "na_g": na_norm_g[0], "ml_g": ml_norm_g[0],
        "g_ffn": norm_ffn_g[0], "w_router": w_router[0].reshape(KD, P, NE).transpose(1, 0, 2),
        "w_gate": w_gate[0], "w_up": w_up[0], "w_down": w_down[0], "g_final": final_norm_g,
    }
    nc = bacc.Bacc("TRN2", target_bir_lowering=False, num_devices=1)
    arrays, t = {}, {}
    for name, a in ins.items():
        arrays["in_" + name] = a = np.ascontiguousarray(a)
        t[name] = nc.dram_tensor("in_" + name, a.shape, F32, kind="ExternalInput").ap()
    for name, shape in SCRATCH.items():
        t[name] = nc.dram_tensor("scr_" + name, shape, F32, kind="Internal").ap()
    t["out"] = nc.dram_tensor("out", (SEQ, D), F32, kind="ExternalOutput").ap()
    trunk(nc, t)
    r = run_bass_kernel_spmd(nc, [arrays], core_ids=[0])
    return r.results[0]["out"].reshape(1, SEQ, D)
```
